# Optimizing a Trainium2 kernel written in Bass

```python
import jax, jax.numpy as jnp
from jax import lax
import numpy as np

D_MODEL = 1024
BATCH = 1
SEQ = 512
DEPTH = 1
DEC_BATCH = 1
DEC_SEQ = 32
PAST_LEN = 256

CHUNK = 64
N_META = 16
D_CONV = D_MODEL
CONV_K = 31
N_HEADS = 16
HEAD_DIM = D_MODEL // N_HEADS
D_ATTN = N_HEADS * HEAD_DIM
D_FF = 4 * D_MODEL
Q_BLOCK = 128
EPS = 1e-6
ATTN_SCALE = HEAD_DIM ** -0.5
OFF_Q = 2 * D_CONV
OFF_K = OFF_Q + D_ATTN
OFF_V = OFF_K + D_ATTN
OFF_G = OFF_V + D_ATTN
D_IN = OFF_G + 2 * D_MODEL

kernel_name = "stickbreak_conformer_hybrid_step"

def _rmsnorm(x, g):
    xf = x.astype(jnp.float32)
    y = xf * lax.rsqrt(jnp.mean(xf * xf, axis=-1, keepdims=True) + EPS)
    return (y * g.astype(jnp.float32)).astype(x.dtype)

def _layernorm(x, g, b):
    xf = x.astype(jnp.float32)
    xc = xf - jnp.mean(xf, axis=-1, keepdims=True)
    var = jnp.mean(xc * xc, axis=-1, keepdims=True)
    y = xc * lax.rsqrt(var + EPS) * g.astype(jnp.float32) + b.astype(jnp.float32)
    return y.astype(x.dtype)

def _in_proj(h, w_in):
    p = h @ w_in
    lead = p.shape[:-1]
    glu = p[..., :D_CONV] * jax.nn.sigmoid(p[..., D_CONV:OFF_Q])
    q = p[..., OFF_Q:OFF_K].reshape(*lead, N_HEADS, HEAD_DIM)
    k = p[..., OFF_K:OFF_V].reshape(*lead, N_HEADS, HEAD_DIM)
    v = p[..., OFF_V:OFF_G].reshape(*lead, N_HEADS, HEAD_DIM)
    return glu, q, k, v, p[..., OFF_G:]

def _conv_branch(ctx, w_dw, b_dw, g_ln, b_ln, w_pw2):
    y = lax.conv_general_dilated(ctx, w_dw[:, None, :].astype(ctx.dtype), window_strides=(1,), padding='VALID',
                                 dimension_numbers=('NWC', 'WIO', 'NWC'), feature_group_count=D_CONV)
    y = y + b_dw
    return jax.nn.silu(_layernorm(y, g_ln, b_ln)) @ w_pw2

def _stick_breaking(q, k, v, q_pos, k_pos):
    z = jnp.einsum('bqhd,bkhd->bhqk', q.astype(jnp.float32), k.astype(jnp.float32)) * ATTN_SCALE
    mask = k_pos[None, :] < q_pos[:, None]
    log_1m = jnp.where(mask, jax.nn.log_sigmoid(-z), 0.0)
    tail = lax.cumsum(log_1m, axis=3, reverse=True) - log_1m
    a = jnp.where(mask, jnp.exp(jax.nn.log_sigmoid(z) + tail), 0.0)
    return jnp.einsum('bhqk,bkhd->bqhd', a, v.astype(jnp.float32)).astype(v.dtype)

def _sb_prompt(q, k, v):
    B, T = q.shape[:2]
    n_blk = -(-T // Q_BLOCK)
    pad = n_blk * Q_BLOCK - T
    q_blocks = jnp.pad(q, ((0, 0), (0, pad), (0, 0), (0, 0)))
    q_blocks = q_blocks.reshape(B, n_blk, Q_BLOCK, N_HEADS, HEAD_DIM).transpose(1, 0, 2, 3, 4)
    k_pos = jnp.arange(T, dtype=jnp.int32)
    starts = jnp.arange(n_blk, dtype=jnp.int32) * Q_BLOCK

    def one_block(args):
        qb, s0 = args
        return _stick_breaking(qb, k, v, s0 + jnp.arange(Q_BLOCK, dtype=jnp.int32), k_pos)

    out = lax.map(one_block, (q_blocks, starts))
    out = out.transpose(1, 0, 2, 3, 4).reshape(B, n_blk * Q_BLOCK, N_HEADS, HEAD_DIM)
    return out[:, :T]

def _merge(conv_out, attn_out, gates, w_out):
    g_conv = jax.nn.sigmoid(gates[..., :D_MODEL])
    g_attn = jax.nn.sigmoid(gates[..., D_MODEL:])
    mixed = g_conv * conv_out + g_attn * attn_out.reshape(*attn_out.shape[:-2], D_ATTN)
    return mixed @ w_out

def _mlp(x, g, w_up, w_down):
    h = _rmsnorm(x, g)
    return jnp.square(jax.nn.relu(h @ w_up)) @ w_down

def _prompt_layer(x, g_mix, w_in, w_dw, b_dw, g_ln, b_ln, w_pw2, w_out, g_mlp, w_up, w_down):
    glu, q, k, v, gates = _in_proj(_rmsnorm(x, g_mix), w_in)
    ctx = jnp.pad(glu, ((0, 0), (CONV_K - 1, 0), (0, 0)))
    conv_out = _conv_branch(ctx, w_dw, b_dw, g_ln, b_ln, w_pw2)
    attn_out = _sb_prompt(q, k, v)
    x = x + _merge(conv_out, attn_out, gates, w_out)
    x = x + _mlp(x, g_mlp, w_up, w_down)
    return x, k, v, glu[:, -(CONV_K - 1):]

def _sample_layer(x, meta_x, cache_k, cache_v, cache_conv,
                  g_mix, w_in, w_dw, b_dw, g_ln, b_ln, w_pw2, w_out, g_mlp, w_up, w_down):
    B, S, _ = x.shape
    P = cache_k.shape[1]
    glu, q, k, v, gates = _in_proj(_rmsnorm(x, g_mix), w_in)
    ctx = jnp.concatenate([cache_conv.astype(glu.dtype), glu], axis=1)
    conv_out = _conv_branch(ctx, w_dw, b_dw, g_ln, b_ln, w_pw2)
    kv_meta = _rmsnorm(meta_x, g_mix) @ w_in[:, OFF_K:OFF_G]
    k_meta = jnp.broadcast_to(kv_meta[:, :D_ATTN].reshape(1, N_META, N_HEADS, HEAD_DIM), (B, N_META, N_HEADS, HEAD_DIM))
    v_meta = jnp.broadcast_to(kv_meta[:, D_ATTN:].reshape(1, N_META, N_HEADS, HEAD_DIM), (B, N_META, N_HEADS, HEAD_DIM))
    k_all = jnp.concatenate([k_meta.astype(k.dtype), cache_k.astype(k.dtype), k], axis=1)
    v_all = jnp.concatenate([v_meta.astype(v.dtype), cache_v.astype(v.dtype), v], axis=1)
    L = N_META + P + S
    q_pos = N_META + P + jnp.arange(S, dtype=jnp.int32)
    attn_out = _stick_breaking(q, k_all, v_all, q_pos, jnp.arange(L, dtype=jnp.int32))
    x = x + _merge(conv_out, attn_out, gates, w_out)
    x = x + _mlp(x, g_mlp, w_up, w_down)
    return x, k, v, ctx[:, -(CONV_K - 1):]

def setup_inputs(seed: int = 0) -> dict:
    key = jax.random.key(seed)
    ks = jax.random.split(key, 20)
    nrm = jax.random.normal
    f32 = jnp.float32
    return {
        "x_prompt": nrm(ks[0], (BATCH, SEQ, D_MODEL), f32),
        "x_sample": nrm(ks[1], (DEC_BATCH, DEC_SEQ, D_MODEL), f32),
        "cache_k": nrm(ks[2], (DEPTH, DEC_BATCH, PAST_LEN, N_HEADS, HEAD_DIM), f32),
        "cache_v": nrm(ks[3], (DEPTH, DEC_BATCH, PAST_LEN, N_HEADS, HEAD_DIM), f32),
        "cache_conv": 0.5 * nrm(ks[4], (DEPTH, DEC_BATCH, CONV_K - 1, D_CONV), f32),
        "meta": nrm(ks[5], (N_META, D_MODEL), f32),
        "g_mix": 1.0 + 0.1 * nrm(ks[6], (DEPTH, D_MODEL), f32),
        "w_in": nrm(ks[7], (DEPTH, D_MODEL, D_IN), f32) * D_MODEL ** -0.5,
        "w_dw": nrm(ks[8], (DEPTH, CONV_K, D_CONV), f32) * CONV_K ** -0.5,
        "b_dw": 0.02 * nrm(ks[9], (DEPTH, D_CONV), f32),
        "g_ln_conv": 1.0 + 0.1 * nrm(ks[10], (DEPTH, D_CONV), f32),
        "b_ln_conv": 0.02 * nrm(ks[11], (DEPTH, D_CONV), f32),
        "w_pw2": nrm(ks[12], (DEPTH, D_CONV, D_MODEL), f32) * D_CONV ** -0.5,
        "w_out": nrm(ks[13], (DEPTH, D_MODEL, D_MODEL), f32) * D_MODEL ** -0.5,
        "g_mlp": 1.0 + 0.1 * nrm(ks[14], (DEPTH, D_MODEL), f32),
        "w_up": nrm(ks[15], (DEPTH, D_MODEL, D_FF), f32) * D_MODEL ** -0.5,
        "w_down": nrm(ks[16], (DEPTH, D_FF, D_MODEL), f32) * D_FF ** -0.5,
        "g_final": 1.0 + 0.1 * nrm(ks[17], (D_MODEL,), f32),
    }

def reference(x_prompt, x_sample, cache_k, cache_v, cache_conv, meta, g_mix, w_in, w_dw, b_dw,
              g_ln_conv, b_ln_conv, w_pw2, w_out, g_mlp, w_up, w_down, g_final):
    assert x_sample.shape[1] <= CHUNK
    B = x_prompt.shape[0]
    meta_p = jnp.broadcast_to(meta.astype(x_prompt.dtype)[None], (B, N_META, D_MODEL))
    xp = jnp.concatenate([meta_p, x_prompt], axis=1)
    xs = x_sample
    meta_x = meta.astype(x_sample.dtype)
    kp, vp, cp, ks_, vs_, cs_ = [], [], [], [], [], []
    for l in range(DEPTH):
        layer_w = (g_mix[l], w_in[l], w_dw[l], b_dw[l], g_ln_conv[l], b_ln_conv[l],
                   w_pw2[l], w_out[l], g_mlp[l], w_up[l], w_down[l])
        xp, k_l, v_l, c_l = _prompt_layer(xp, *layer_w)
        kp.append(k_l); vp.append(v_l); cp.append(c_l)
        xs, k_l, v_l, c_l = _sample_layer(xs, meta_x, cache_k[l], cache_v[l], cache_conv[l], *layer_w)
        ks_.append(k_l); vs_.append(v_l); cs_.append(c_l)
        if l + 1 < DEPTH:
            meta_x = _prompt_layer(meta_x[None], *layer_w)[0][0]
    y_prompt = _rmsnorm(xp, g_final)[:, N_META:]
    y_sample = _rmsnorm(xs, g_final)
    new_k_prompt = jnp.stack(kp)
    new_v_prompt = jnp.stack(vp)
    new_conv_prompt = jnp.stack(cp)
    new_k_sample = jnp.stack(ks_)
    new_v_sample = jnp.stack(vs_)
    new_conv_sample = jnp.stack(cs_)
    return (y_prompt, y_sample, new_k_prompt, new_v_prompt, new_conv_prompt, new_k_sample, new_v_sample, new_conv_sample)


_drawn_inputs = setup_inputs


def setup_inputs(seed=0):
    import zlib

    import numpy as np

    out = dict(_drawn_inputs(seed))
    spreads = {}
    factors = {'b_dw': 4.637, 'b_ln_conv': 8.0}
    for name, (base, spread) in spreads.items():
        noise = np.random.default_rng([zlib.crc32(name.encode()), seed]).standard_normal(out[name].shape)
        drawn = base * np.exp(spread * noise) if base else spread * noise
        out[name] = __import__('jax').numpy.asarray(drawn.astype(out[name].dtype))
    for name, factor in factors.items():
        out[name] = (out[name] * factor).astype(out[name].dtype)
    return out
```

```python
from contextlib import ExitStack

import concourse.bass as bass
from concourse import mybir

P = 128
ACT = mybir.ActivationFunctionType
ALU = mybir.AluOpType
F32 = mybir.dt.float32
F32R = mybir.dt.float32r
BF16 = mybir.dt.bfloat16

D = 1024
KC = D // P
HEADS, HD = 16, 64
META, SEQ, DEC = 16, 512, 32
PAST = 256
TAPS = 31
PAD = TAPS - 1
FF = 4 * D
EPS = 1e-6
TOK = META + SEQ + DEC
OUTTOK = SEQ + DEC
HALF, HALFO = TOK // 2, OUTTOK // 2
KEYS = 5 * P
NEG = -1e30

LOOP_UNITS = 6
N_LOOP = KC * LOOP_UNITS
RING_LOOP, RING = 3, 4
GROUPS_PER_STAGE = KC // 4
ROUNDS = 4
N_GROUPS = (3 + 2 * ROUNDS) * GROUPS_PER_STAGE

T_A, T_B, T_Q, T_CT, T_K, T_V, T_VT, T_G, T_KT, T_GT = range(10)
LOOP_TILES = 10
FIRST_POST = KC + KC * LOOP_TILES

KT = [(0, 0, 512, 0), (1, 0, 400, 112), (2, 0, 272, 240), (2, 272, 144, 368), (1, 400, 16, 496)]
S_CACHE0, S_CACHE1, S_OWN = (2, 416), (2, 448), (2, 480)
BANK_COLS = (512, 416, 512)
S_PV = 416


def build(nc, x_prompt, x_sample, cache_k, cache_v, cache_conv, meta, g_mix, w_in, w_dw, b_dw,
          g_ln_conv, b_ln_conv, w_pw2, w_out, g_mlp, w_up, w_down, g_final,
          y_prompt, y_sample, new_k_prompt, new_v_prompt, new_conv_prompt,
          new_k_sample, new_v_sample, new_conv_sample):
    xp, xs = x_prompt[0], x_sample[0]

    def weight(w, name):
        return w.rearrange("(k p) (n c) -> p k n c", p=P, c=P)

    win_v = weight(w_in[0], "in")
    wpw_v = weight(w_pw2[0], "pw2")
    wout_v = weight(w_out[0], "out")
    wup_v = weight(w_up[0], "up")
    wdown_v = w_down[0].rearrange("(r k p) (n c) -> p r k n c", p=P, k=KC, c=P)
    ck_v = cache_k[0, 0].rearrange("(t p) h d -> p t (h d)", p=P).rearrange("p t (n c) -> p t n c", c=P)
    cv_v = cache_v[0, 0].rearrange("(t p) h d -> p t (h d)", p=P).rearrange("p t (n c) -> p t n c", c=P)

    def rows(o):
        return o[0, 0].rearrange("t h d -> t (h d)").rearrange("t (n c) -> t n c", c=P)

    nkp, nvp, nks, nvs = rows(new_k_prompt), rows(new_v_prompt), rows(new_k_sample), rows(new_v_sample)
    ncp = new_conv_prompt[0, 0].rearrange("t (n c) -> t n c", c=P)
    ncs = new_conv_sample[0, 0].rearrange("t (n c) -> t n c", c=P)

    with ExitStack() as ctx:
        def sb(name, shape, dt=F32, where=ctx):
            return where.enter_context(nc.sbuf_tensor(name, shape, dt))

        def sem(name):
            return ctx.enter_context(nc.semaphore(name))

        w_raw = sb("w_raw", [P, RING, KC, P])
        w_hi = sb("w_hi", [P, RING, KC, P], F32R)
        w_lo = sb("w_lo", [P, RING, KC, P], F32R)
        xT = sb("xT", [P, KC, TOK])
        r_hi = sb("r_hi", [P, KC, TOK], F32R)
        r_lo = sb("r_lo", [P, KC, TOK], F32R)
        ident = sb("ident", [P, P])
        ident_b = sb("ident_b", [P, P], BF16)
        ones = sb("ones", [P, P])
        tri = sb("tri", [P, P], F32R)
        negones = sb("negones", [P, P], F32R)
        own_all = sb("own_all", [P, P], F32R)
        own_own = sb("own_own", [P, P], F32R)
        cache_meta = sb("cache_meta", [P, P], F32R)
        neg_diag = sb("neg_diag", [P, P], BF16)
        neg_own = sb("neg_own", [P, DEC], BF16)
        cw = sb("cw", [P, KC, PAD + TAPS])
        vecs = sb("vecs", [P, 6 * KC])
        eps_col = sb("eps_col", [P, 1])
        rstd = sb("rstd", [P, TOK])
        n32 = sb("n32", [P, 2, TOK])

        sq = n32

        def vec(n, k):
            return vecs[:, n * KC + k:n * KC + k + 1]
        G_MIX, B_DW, G_LN, B_LN, G_MLP, G_FINAL = range(6)

        mid = ExitStack()
        yconv = sb("yconv", [P, KC, OUTTOK], where=mid)
        mixed = sb("mixed", [P, KC, OUTTOK], where=mid)
        sum_y = sb("sum_y", [P, OUTTOK], where=mid)

        loop = ExitStack()
        qT = sb("qT", [P, OUTTOK], where=loop)
        kT = sb("kT", [P, KEYS], where=loop)
        vT = sb("vT", [P, KEYS], where=loop)
        v_tok = sb("v_tok", [P, 5, P], where=loop)
        k_tok = sb("k_tok", [P, 5, P], where=loop)
        glu_tok = sb("glu_tok", [92, P], where=loop)
        ck_tok = sb("ck_tok", [P, 2, P], where=loop)
        cv_tok = sb("cv_tok", [P, 2, P], where=loop)
        ckT = sb("ckT", [P, 2 * P], where=loop)
        CTX_CACHE = PAD + META + SEQ
        CTX_S = CTX_CACHE + PAD
        CONV_COLS = CTX_S + DEC - META - PAD
        conv_in = sb("conv_in", [P, CTX_S + DEC], where=loop)
        acc = sb("acc", [P, 2, CONV_COLS], where=loop)
        cw_cur = sb("cw_cur", [P, PAD + TAPS], where=loop)
        bdw_cur = sb("bdw_cur", [P, 1], where=loop)
        a_sb = sb("a_sb", [P, TOK], where=loop)
        gate_b = sb("gate_b", [P, TOK], where=loop)
        gate_a = sb("gate_a", [P, OUTTOK], where=loop)
        attn = ExitStack()
        ez = sb("ez", [P, 3, 512], where=attn)
        sp = sb("sp", [P, 3, 512], where=attn)
        sp_hi = sb("sp_hi", [P, 3, 512], F32R, where=attn)
        sp_lo = sb("sp_lo", [P, 3, 512], F32R, where=attn)
        prob = ez
        attn.close()
        start = ExitStack()
        x_tok = sb("x_tok", [P, 5, D], where=start)
        cw_rows = sb("cw_rows", [PAD + TAPS, D], where=start)
        vec_rows = sb("vec_rows", [6 * KC, P], where=start)
        mat_f = sb("mat_f", [P, 5, P], where=start)
        start.close()
        loop.close()

        post = ExitStack()
        gate_c = sb("gate_c", [P, KC, OUTTOK], where=post)
        s_hi = sb("s_hi", [P, KC, OUTTOK], F32R, where=post)
        s_lo = sb("s_lo", [P, KC, OUTTOK], F32R, where=post)
        part = sb("part", [P, 2, OUTTOK], where=post)
        sum_sq = sb("sum_sq", [P, OUTTOK], where=post)
        post.close()
        mid.close()

        u_hi = sb("u_hi", [P, 2, KC, OUTTOK], F32R)
        u_lo = sb("u_lo", [P, 2, KC, OUTTOK], F32R)

        dense = ctx.enter_context(nc.psum_tensor("dense", [P, 2, 2, 512], F32))
        z = ctx.enter_context(nc.psum_tensor("z", [P, 3, 512], F32))
        pv = ctx.enter_context(nc.psum_tensor("pv", [P, 512], F32))

        x_loaded = sem("x_loaded")
        rows_loaded = sem("rows_loaded")
        raw_loop = [sem(f"raw_loop{n}") for n in range(LOOP_UNITS)]
        raw_post = [sem(f"raw_post{n}") for n in range(4)]
        ck_loaded, cv_loaded = sem("ck_loaded"), sem("cv_loaded")
        hi_done, lo_done = sem("hi_done"), sem("lo_done")
        tile_done = sem("tile_done")
        emptied = [sem("emptied0"), sem("emptied1")]
        consts, mats = sem("consts"), sem("mats")
        rows_turned, rows_kept = sem("rows_turned"), sem("rows_kept")
        sq_done, ss_done = sem("sq_done"), sem("ss_done")
        eps_set, mean_kept = sem("eps_set"), sem("mean_kept")
        ln_step, rstd_done = sem("ln_step"), sem("rstd_done")
        n32_done, nhi_done, r_ready = sem("n32_done"), sem("nhi_done"), sem("r_ready")
        cur_done = sem("cur_done")
        a_kept, gb_abs, gb_exp, gb_ln, gb_log, gb_done = (sem(n) for n in ("a_kept", "gb_abs", "gb_exp", "gb_ln", "gb_log", "gb_done"))
        ga_abs, ga_exp, ga_ln, ga_log, ga_done = (sem(n) for n in ("ga_abs", "ga_exp", "ga_ln", "ga_log", "ga_done"))
        glu_done, tap_done, y_done = sem("glu_done"), sem("tap_done"), sem("y_done")
        q_kept, ckT_kept, k_kept, v_kept = sem("q_kept"), sem("ckT_kept"), sem("k_kept"), sem("v_kept")
        vtok_kept, ktok_kept, glutok_kept = sem("vtok_kept"), sem("ktok_kept"), sem("glutok_kept")
        z_scored, abs_done, exp_done, log_done = sem("z_scored"), sem("abs_done"), sem("exp_done"), sem("log_done")
        sp_done, sphi_done, splo_done = sem("sp_done"), sem("sphi_done"), sem("splo_done")
        cum_done, prob_done, pv_done, mix_done = sem("cum_done"), sem("prob_done"), sem("pv_done"), sem("mix_done")
        kv_out = sem("kv_out")
        sumy_done, mean_done, centred, ysq_done, ssum_done = (sem(n) for n in ("sumy_done", "mean_done", "centred", "ysq_done", "ssum_done"))
        var_done, u_done, silu_done, s_ready = (sem(n) for n in ("var_done", "u_done", "silu_done", "s_ready"))
        m_done, mhi_done, m_ready = (sem(n) for n in ("m_done", "mhi_done", "m_ready"))
        x2sq_done, x2sum_done, ss2_done = (sem(n) for n in ("x2sq_done", "x2sum_done", "ss2_done"))
        h2_ready, u32_done, uhi_done, u_ready = (sem(n) for n in ("h2_ready", "u32_done", "uhi_done", "u_ready"))
        fin_done = sem("fin_done")
        ytok_kept = [sem("ytok_kept0"), sem("ytok_kept1")]
        y_out = [sem("y_out0"), sem("y_out1")]
        zeroed = sem("zeroed")

        def y_rows(s):
            return w_raw[:, 2 * s].rearrange("p k c -> p (k c)")

        def tile(i, t):
            return KC + LOOP_TILES * i + t

        UNIT_TILE = (T_A, T_B, T_Q, T_K, T_V, T_G)

        def emptied_at(g, n):
            return KC // 2 + 2 * g + n // 2 + 1

        def psum2(slot, half):
            return dense[:, slot, :, 0:half]

        def cols2(ap, half):
            return ap.rearrange("p (h c) -> p h c", c=half)

        block = ctx.enter_context(nc.Block())

        @block.sync
        def _(sync):
            for dst, src in ((x_tok[0:META, 0, :], meta), (x_tok[META:P, 0, :], xp[0:P - META]),
                             (x_tok[:, 1:4, :], xp[P - META:4 * P - META].rearrange("(t p) d -> p t d", p=P)),
                             (x_tok[0:META, 4, :], xp[4 * P - META:SEQ]), (x_tok[META:META + DEC, 4, :], xs)):
                sync.dma_start(dst, src).then_inc(x_loaded, 16)
            for n, v in enumerate((g_mix, b_dw, g_ln_conv, b_ln_conv, g_mlp)):
                sync.dma_start(vec_rows[n * KC:(n + 1) * KC, :], v[0].rearrange("(k p) -> k p", p=P)).then_inc(rows_loaded, 16)
            sync.dma_start(vec_rows[5 * KC:, :], g_final.rearrange("(k p) -> k p", p=P)).then_inc(rows_loaded, 16)
            sync.dma_start(cw_rows[0:PAD, :], cache_conv[0, 0]).then_inc(rows_loaded, 16)
            sync.dma_start(cw_rows[PAD:, :], w_dw[0]).then_inc(rows_loaded, 16)

            BASE = [0, KC, 2 * KC, 3 * KC, 4 * KC, 6 * KC]

            def loads(i, first):
                for u in range(LOOP_UNITS):
                    if not (first and u < RING_LOOP):
                        sync.wait_ge(lo_done, LOOP_UNITS * i + u - 2)
                    sync.dma_start(w_raw[:, u % RING_LOOP], win_v[:, :, bass.ds(BASE[u] + i, 1), :].rearrange("p k n c -> p k (n c)")).then_inc(raw_loop[u], 16)
                    if u == 0:
                        if not first:
                            sync.wait_ge(ckT_kept, i)
                        sync.dma_start(ck_tok[:], ck_v[:, :, bass.ds(i, 1), :].rearrange("p t n c -> p t (n c)")).then_inc(ck_loaded, 16)
                    if u == 4:
                        if not first:
                            sync.wait_ge(pv_done, 2 * i)
                        sync.dma_start(cv_tok[:], cv_v[:, :, bass.ds(i, 1), :].rearrange("p t n c -> p t (n c)")).then_inc(cv_loaded, 16)

            loads(0, True)
            with sync.Fori(1, KC) as i:
                loads(i, False)

            for n in range(4):
                sync.wait_ge(lo_done, N_LOOP + n - 2)
                sync.dma_start(w_raw[:, n], win_v[:, :, 5 * KC + n, :]).then_inc(raw_loop[n] if n < 2 else raw_post[n], 16)

            def load_group(g, view):
                for n in range(4):
                    sync.wait_ge(lo_done, N_LOOP + 4 * g + n - 3)
                    sync.dma_start(w_raw[:, n], view(n)).then_inc(raw_post[n], 16)

            load_group(1, lambda n: win_v[:, :, 5 * KC + 4 + n, :])
            for first_group, view in ((2, wpw_v), (4, wout_v)):
                with sync.Fori(0, 2) as j:
                    load_group(first_group + j, lambda n: view[:, :, bass.ds(4 * j + n, 1), :].rearrange("p k n c -> p k (n c)"))
            with sync.Fori(0, 2) as rr:
                with sync.Fori(0, 4) as j:
                    load_group(6 + 8 * rr + j, lambda n: wup_v[:, :, bass.ds(16 * rr + 4 * j + n, 1), :].rearrange("p k n c -> p k (n c)"))
                for half in range(2):
                    with sync.Fori(0, 2) as j:
                        load_group(10 + 2 * half + 8 * rr + j, lambda n: wdown_v[:, bass.ds(2 * rr + half, 1), :, bass.ds(4 * j + n, 1), :].rearrange("p r k n c -> p (r k) (n c)"))

            for t in range(5):
                sync.wait_ge(ytok_kept[t % 2], t // 2 + 1)
                if t < 4:
                    sync.dma_start(y_prompt[0, t * P:(t + 1) * P, :], y_rows(t % 2)).then_inc(y_out[t % 2], 16)
                else:
                    sync.dma_start(y_sample[0], y_rows(0)[0:DEC, :]).then_inc(y_out[0], 16)
            sync.wait_ge(y_out[0], 16 * 3)
            sync.wait_ge(y_out[1], 16 * 2)

        @block.gpsimd
        def _(pool):
            pool.memset(ident[:], 0.0).then_inc(consts, 1)
            pool.memset(ones[:], 1.0).then_inc(consts, 1)
            pool.memset(neg_diag[:], 0.0).then_inc(consts, 1)
            pool.memset(neg_own[:], 0.0).then_inc(consts, 1)
            pool.memset(mat_f[:], -1.0).then_inc(consts, 1)
            pool.memset(kT[:, TOK + META:KEYS], 0.0).then_inc(zeroed, 1)
            pool.memset(vT[:, TOK + META:KEYS], 0.0).then_inc(zeroed, 1)
            pool.memset(conv_in[:, 0:PAD], 0.0).then_inc(zeroed, 1)
            pool.memset(sum_y[:], 0.0).then_inc(zeroed, 1)
            done = 5

            def select(ap, pattern, base, mult, fill, op=ALU.is_ge):
                nonlocal done
                pool.wait_ge(consts, done)
                pool.affine_select(out=ap, in_=ap, pattern=pattern, compare_op=op, fill=fill, base=base, channel_multiplier=mult).then_inc(consts, 1)
                done += 1

            select(ident[:], [[-1, P]], 0, 1, 1.0, ALU.not_equal)
            select(neg_diag[:], [[1, P]], -1, -1, NEG)
            select(neg_own[:], [[1, DEC]], META - 1, -1, NEG)
            select(neg_own[:], [[0, DEC]], META + DEC - 1, -1, 0.0)
            select(neg_own[:], [[0, DEC]], META + DEC + META - 1, -1, NEG)
            select(neg_own[:], [[0, DEC]], -META, 1, NEG)
            M0 = META + DEC
            select(mat_f[:, 0, :], [[-1, P]], 0, 1, 0.0)
            select(mat_f[:, 2, :], [[0, P]], M0 - 1, -1, 0.0)
            select(mat_f[:, 3, 0:M0], [[-1, M0]], 0, 1, 0.0)
            select(mat_f[:, 3, 0:M0], [[0, M0]], M0 - 1, -1, 0.0)
            select(mat_f[:, 3, M0:P], [[0, P - M0]], M0 - 1, -1, 0.0)
            select(mat_f[:, 3, M0:P], [[1, P - M0]], M0 - 1, -1, -1.0)
            select(mat_f[:, 4, :], [[1, P]], -M0, 0, 0.0)
            pool.wait_ge(consts, done)
            pool.tensor_copy(ident_b[:], ident[:]).then_inc(mats, 1)
            for n, m in enumerate((tri, negones, own_all, own_own, cache_meta)):
                pool.tensor_copy(m[:], mat_f[:, n, :]).then_inc(mats, 1)

            def low(u, s):
                pool.wait_ge(hi_done, u + 1)
                pool.tensor_tensor(w_lo[:, s], w_raw[:, s], w_hi[:, s].bitcast(F32), ALU.subtract).then_inc(lo_done, 1)

            with pool.Fori(0, N_LOOP // RING_LOOP) as j:
                for s in range(RING_LOOP):
                    low(RING_LOOP * j + s, s)
            with pool.Fori(0, N_GROUPS) as g:
                for s in range(RING):
                    low(N_LOOP + RING * g + s, s)

        @block.tensor
        def _(pe):
            def claim(slot, n):
                pe.wait_ge(emptied[slot], n)

            def dense_unit(wslot, slot, m_hi, m_lo, c0, half, chunk_ready=None):
                for k in range(KC):
                    if chunk_ready is not None:
                        pe.wait_ge(chunk_ready[0], chunk_ready[1] + k)
                    for n, (w, m) in enumerate(((w_hi, m_hi), (w_hi, m_lo), (w_lo, m_hi))):
                        for h in range(2):
                            mm = nc.tensor.matmul(dense[:, slot, h, 0:half], w[:, wslot, k, :], m[:, k, c0 + h * half:c0 + (h + 1) * half],
                                                  start=(k == 0 and n == 0), stop=(k == KC - 1 and n == 2))
                mm.then_inc(tile_done, 1)

            pe.wait_ge(consts, 18)
            pe.wait_ge(rows_loaded, 16 * 8)
            for k in range(KC):
                nc.tensor.transpose(z[:, 0, k * 61:(k + 1) * 61], cw_rows[:, k * P:(k + 1) * P], ident[0:61, 0:61])
            nc.tensor.transpose(z[:, 1, 0:6 * KC], vec_rows[:], ident[0:6 * KC, 0:6 * KC]).then_inc(rows_turned, 1)
            pe.wait_ge(x_loaded, 16 * 5)

            def x_squares(k):
                pe.wait_ge(sq_done, k + 1)
                for h in range(2):
                    mm = nc.tensor.matmul(z[:, h, 0:HALF], ones[:], sq[:, k % 2, h * HALF:(h + 1) * HALF], start=(k == 0), stop=(k == KC - 1))
                mm.then_inc(ss_done, 1)

            for k in range(KC):
                if k >= 2:
                    claim(k % 2, k // 2)
                for t in range(5):
                    n = P if t < 4 else META + DEC
                    mm = nc.tensor.transpose(dense[:, k % 2, t // 4, (t % 4) * P:(t % 4) * P + n], x_tok[0:n, t, k * P:(k + 1) * P], ident[0:n, 0:n])
                mm.then_inc(tile_done, 1)
                if k >= 1:
                    if k == 1:
                        pe.wait_ge(rows_kept, 2)
                    x_squares(k - 1)
            x_squares(KC - 1)
            pe.wait_ge(mats, 6)

            def scores(i, hh):
                r = slice(hh * HD, (hh + 1) * HD)
                head = 2 * i + hh
                if hh == 0:
                    pe.wait_ge(q_kept, i + 1)
                    pe.wait_ge(k_kept, i + 1)
                    pe.wait_ge(ckT_kept, i + 1)
                else:
                    pe.wait_ge(prob_done, 3 * head)
                for b in range(3):
                    first = True
                    for j, (bank, off, cols, q0) in enumerate(KT):
                        if bank != b:
                            continue
                        nc.tensor.matmul(z[:, b, off:off + cols], kT[r, j * P:(j + 1) * P], qT[r, q0:SEQ], start=first, stop=False, skip_group_check=True)
                        first = False
                        lo, n = (META, P - META) if j == 0 else (0, min(P, cols))
                        mm = nc.tensor.matmul(z[:, b, off:off + n], ident_b[:], neg_diag[:, lo:lo + n], start=False, stop=False, skip_group_check=True)
                    if b == 2:
                        for (_, off), keys in ((S_CACHE0, ckT[r, 0:P]), (S_CACHE1, ckT[r, P:2 * P]), (S_OWN, kT[r, 4 * P:5 * P])):
                            nc.tensor.matmul(z[:, b, off:off + DEC], keys, qT[r, SEQ:OUTTOK], start=False, stop=False, skip_group_check=True)
                        mm = nc.tensor.matmul(z[:, b, S_OWN[1]:S_OWN[1] + DEC], ident_b[:], neg_own[:], start=False, stop=False, skip_group_check=True)
                    mm.then_inc(z_scored, 1)

            def cumulate(head):
                def add(m, db, doff, n, sbk, soff):
                    for part_ in (sp_hi, sp_lo):
                        mm = nc.tensor.matmul(z[:, db, doff:doff + n], m[:], part_[:, sbk, soff:soff + n], start=False, stop=False, skip_group_check=True)
                    return mm
                pe.wait_ge(splo_done, 3 * head + 1)
                add(tri, 0, 0, 512, 0, 0)
                pe.wait_ge(splo_done, 3 * head + 3)
                for j in range(1, 5):
                    sbk, soff, n, sq0 = KT[j]
                    for jj in range(j + 1):
                        db, doff, _, dq0 = KT[jj]
                        mm = add(tri if jj == j else negones, db, doff + sq0 - dq0, n, sbk, soff)
                for m, dst, src in ((tri, S_CACHE0, S_CACHE0), (cache_meta, S_OWN, S_CACHE0), (tri, S_CACHE1, S_CACHE1),
                                    (negones, S_CACHE0, S_CACHE1), (cache_meta, S_OWN, S_CACHE1), (own_own, S_OWN, S_OWN),
                                    (own_all, S_CACHE0, S_OWN), (own_all, S_CACHE1, S_OWN)):
                    mm = add(m, dst[0], dst[1], DEC, src[0], src[1])
                mm.then_inc(cum_done, 1)

            def values(i, hh):
                r = slice(hh * HD, (hh + 1) * HD)
                head = 2 * i + hh
                if hh == 0:
                    pe.wait_ge(vtok_kept, i + 1)
                    pe.wait_ge(cv_loaded, 16 * (i + 1))
                pe.wait_ge(prob_done, 3 * head + 1)
                for n, j in enumerate((0, 1, 4, 2, 3)):
                    bank, off, cols, q0 = KT[j]
                    if n == 1:
                        pe.wait_ge(prob_done, 3 * head + 2)
                    if n == 3:
                        pe.wait_ge(prob_done, 3 * head + 3)
                    nc.tensor.matmul(pv[r, q0:SEQ], v_tok[:, j, r], prob[:, bank, off:off + cols], start=(n == 0), stop=(n == 4), skip_group_check=True)
                for n, ((bank, off), v) in enumerate(((S_CACHE0, cv_tok[:, 0, r]), (S_CACHE1, cv_tok[:, 1, r]), (S_OWN, v_tok[:, 4, r]))):
                    mm = nc.tensor.matmul(z[r, 1, S_PV:S_PV + DEC], v, prob[:, bank, off:off + DEC], start=(n == 0), stop=(n == 2), skip_group_check=True)
                mm.then_inc(pv_done, 1)

            def turn(i):
                read_before = {T_Q: a_kept, T_CT: gb_log, T_K: q_kept, T_V: ckT_kept, T_VT: k_kept,
                               T_G: v_kept, T_KT: vtok_kept, T_GT: ga_log}

                def claim_t(t):
                    if t in read_before:
                        pe.wait_ge(read_before[t], i + 1)

                def unit(u):
                    t = UNIT_TILE[u]
                    pe.wait_ge(lo_done, LOOP_UNITS * i + u + 1)
                    claim_t(t)
                    out_only = u in (2, 5)
                    dense_unit(u % RING_LOOP, t % 2, r_hi, r_lo, META if out_only else 0, HALFO if out_only else HALF,
                               (r_ready, 1) if u == 0 else None)

                unit(0)
                unit(1)
                unit(2)
                claim_t(T_CT)
                pe.wait_ge(ck_loaded, 16 * (i + 1))
                for t in range(2):
                    mm = nc.tensor.transpose(dense[:, 1, 0, t * P:(t + 1) * P], ck_tok[:, t, :], ident[:])
                mm.then_inc(tile_done, 1)
                unit(3)
                scores(i, 0)
                unit(4)
                cumulate(2 * i)
                claim_t(T_VT)
                pe.wait_ge(v_kept, i + 1)
                for t in range(5):
                    mm = nc.tensor.transpose(dense[:, 0, t // 4, (t % 4) * P:(t % 4 + 1) * P], vT[:, t * P:(t + 1) * P], ident[:])
                mm.then_inc(tile_done, 1)
                values(i, 0)
                scores(i, 1)
                unit(5)
                cumulate(2 * i + 1)
                claim_t(T_KT)
                for t in range(5):
                    mm = nc.tensor.transpose(dense[:, 0, t // 4, (t % 4) * P:(t % 4 + 1) * P], kT[:, t * P:(t + 1) * P], ident[:])
                mm.then_inc(tile_done, 1)
                claim_t(T_GT)
                pe.wait_ge(glu_done, i + 1)
                nc.tensor.transpose(dense[0:92, 1, 0, 0:P], conv_in[:, CTX_CACHE - PAD:CTX_S + DEC], ident[:]).then_inc(tile_done, 1)
                values(i, 1)
                pe.wait_ge(ktok_kept, i + 1)
                pe.wait_ge(glutok_kept, i + 1)

            claim(0, KC // 2)
            claim(1, KC // 2)
            with pe.Fori(0, KC) as i:
                turn(i)

            pe.wait_ge(sumy_done, KC)
            for h in range(2):
                mm = nc.tensor.matmul(z[:, h, 0:HALFO], ones[:], sum_y[:, h * HALFO:(h + 1) * HALFO], start=True, stop=True)
            mm.then_inc(mean_done, 1)

            def group(g, m_hi, m_lo, c0, ready=None):
                for n in range(4):
                    pe.wait_ge(lo_done, N_LOOP + 4 * g + n + 1)
                    claim(n % 2, KC // 2 + 2 * g + n // 2)
                    dense_unit(n, n % 2, m_hi, m_lo, c0, HALFO, ready)

            with pe.Fori(0, 2) as g:
                group(g, r_hi, r_lo, META)
            pe.wait_ge(ssum_done, KC)
            for h in range(2):
                mm = nc.tensor.matmul(z[:, h, 0:HALFO], ones[:], sum_sq[:, h * HALFO:(h + 1) * HALFO], start=True, stop=True)
            mm.then_inc(var_done, 1)
            with pe.Fori(2, 4) as g:
                group(g, s_hi, s_lo, 0, (s_ready, 1))
            with pe.Fori(4, 6) as g:
                group(g, r_hi, r_lo, 0, (m_ready, 1))

            def squares(n):
                pe.wait_ge(x2sum_done, n)
                for h in range(2):
                    mm = nc.tensor.matmul(z[:, h, 0:HALFO], ones[:], n32[:, 1, h * HALFO:(h + 1) * HALFO], start=True, stop=True)
                mm.then_inc(ss2_done, 1)

            squares(KC)
            with pe.Fori(0, 2) as rr:
                with pe.Fori(0, 4) as j:
                    group(6 + 8 * rr + j, r_hi, r_lo, 0, (h2_ready, 1))
                for half in range(2):
                    with pe.Fori(0, 2) as j:
                        group(10 + 2 * half + 8 * rr + j, u_hi[:, half], u_lo[:, half], 0, (u_ready, 16 * rr + 8 * half + 1))
            squares(2 * KC)
            pe.wait_ge(fin_done, KC)
            for t in range(5):
                if t < 2:
                    claim(t, KC // 2 + 2 * N_GROUPS)
                else:
                    pe.wait_ge(ytok_kept[t % 2], t // 2)
                n = P if t < 4 else DEC
                for k in range(KC):
                    mm = nc.tensor.transpose(dense[0:n, t % 2, k // 4, (k % 4) * P:(k % 4 + 1) * P], xT[:, k, META + t * P:META + t * P + n], ident[:])
                mm.then_inc(tile_done, 1)

        @block.scalar
        def _(act):
            def high(s, raw_sem, raw_count, free_tile):
                act.wait_ge(raw_sem, raw_count)
                if free_tile is not None:
                    act.wait_ge(tile_done, free_tile)
                nc.scalar.activation(w_hi[:, s], w_raw[:, s], ACT.Copy).then_inc(hi_done, 1)

            act.wait_ge(rows_turned, 1)
            nc.scalar.activation(cw[:].rearrange("p k r -> p (k r)"), z[:, 0, 0:KC * 61], ACT.Copy).then_inc(rows_kept, 1)
            for k in range(KC):
                act.wait_ge(emptied[k % 2], k // 2 + 1)
                if k >= 2:
                    act.wait_ge(ss_done, k - 1)
                nc.scalar.activation(sq[:, k % 2, :], xT[:, k, :], ACT.Square).then_inc(sq_done, 1)
            high(0, raw_loop[0], 16, None)
            high(1, raw_loop[1], 16, None)

            def inverse_root(psum_sem, count, step, cols, half):
                act.wait_ge(psum_sem, count)
                nc.scalar.activation(cols2(rstd[:, 0:cols], half), z[:, 0:2, 0:half], ACT.Ln, scale=1.0 / D, bias=eps_col[:, 0:1]).then_inc(ln_step, 1)
                act.wait_ge(ln_step, step)
                nc.scalar.activation(rstd[:, 0:cols], rstd[:, 0:cols], ACT.Exp, scale=-0.5).then_inc(rstd_done, 1)

            def split_high(n, cols, ready, ready_count, dst, done):
                act.wait_ge(ready, ready_count)
                nc.scalar.activation(dst, n32[:, n % 2, 0:cols], ACT.Copy).then_inc(done, 1)

            act.wait_ge(eps_set, 1)
            inverse_root(ss_done, KC, 1, TOK, HALF)
            for k in range(KC):
                split_high(k, TOK, n32_done, k + 1, r_hi[:, k, :], nhi_done)

            def log_sigmoid_parts(src, dst, half, tile_n, s_abs, s_exp, s_ln, count, free):
                act.wait_ge(tile_done, tile_n)
                nc.scalar.activation(cols2(dst, half), src, ACT.Abs).then_inc(s_abs, 1)
                act.wait_ge(s_abs, count)
                nc.scalar.activation(dst, dst, ACT.Exp, scale=-1.0).then_inc(s_exp, 1)
                act.wait_ge(s_exp, count)
                nc.scalar.activation(dst, dst, ACT.Ln, bias=1.0).then_inc(s_ln, 1)

            def softplus_logs(head):
                for b in range(3):
                    c = BANK_COLS[b]
                    act.wait_ge(z_scored, 3 * head + b + 1)
                    nc.scalar.activation(ez[:, b, 0:c], z[:, b, 0:c], ACT.Abs).then_inc(abs_done, 1)
                for b in range(3):
                    c = BANK_COLS[b]
                    act.wait_ge(abs_done, 3 * head + b + 1)
                    nc.scalar.activation(ez[:, b, 0:c], ez[:, b, 0:c], ACT.Exp, scale=-1.0).then_inc(exp_done, 1)
                for b in range(3):
                    c = BANK_COLS[b]
                    act.wait_ge(exp_done, 3 * head + b + 1)
                    nc.scalar.activation(ez[:, b, 0:c], ez[:, b, 0:c], ACT.Ln, bias=1.0).then_inc(log_done, 1)
                for b in range(3):
                    c = BANK_COLS[b]
                    act.wait_ge(sp_done, 3 * head + b + 1)
                    nc.scalar.activation(sp_hi[:, b, 0:c], sp[:, b, 0:c], ACT.Copy).then_inc(sphi_done, 1)

            def probabilities(head):
                act.wait_ge(cum_done, head + 1)
                for b in range(3):
                    c = BANK_COLS[b]
                    nc.scalar.activation(prob[:, b, 0:c], z[:, b, 0:c], ACT.Exp).then_inc(prob_done, 1)

            def rows_out(buf, prompt, sample, i):
                n = bass.ds(i, 1)
                act.dma_start(prompt[0:4 * P, n, :].rearrange("(t p) n c -> p t (n c)", p=P), buf[:, 0:4, :]).then_inc(kv_out, 16)
                act.dma_start(prompt[4 * P:4 * P + META, n, :].rearrange("t n c -> t (n c)"), buf[0:META, 4, :]).then_inc(kv_out, 16)
                act.dma_start(sample[:, n, :].rearrange("t n c -> t (n c)"), buf[META:META + DEC, 4, :]).then_inc(kv_out, 16)

            def unturn(i, t, slot, dst, kept):
                act.wait_ge(tile_done, tile(i, t) + 1)
                nc.scalar.activation(dst[:, 0:4, :].rearrange("p t c -> p (t c)"), dense[:, slot, 0, :], ACT.Copy)
                nc.scalar.activation(dst[:, 4, :], dense[:, slot, 1, 0:P], ACT.Copy).then_inc(kept, 1)

            def turn(i):
                def high_ahead(u):
                    prev = (u - RING_LOOP) % LOOP_UNITS
                    free = tile(i, UNIT_TILE[prev]) + 1 if u >= RING_LOOP else tile(i, UNIT_TILE[prev]) + 1 - LOOP_TILES
                    high(u % RING_LOOP, raw_loop[u % LOOP_UNITS], 16 * (i + 1 + u // LOOP_UNITS), free)

                high_ahead(2)
                act.wait_ge(tile_done, tile(i, T_A) + 1)
                nc.scalar.activation(cols2(a_sb[:], HALF), psum2(0, HALF), ACT.Copy).then_inc(a_kept, 1)
                high_ahead(3)
                log_sigmoid_parts(psum2(1, HALF), gate_b[:], HALF, tile(i, T_B) + 1, gb_abs, gb_exp, gb_ln, i + 1, None)
                act.wait_ge(gb_log, i + 1)
                nc.scalar.activation(gate_b[:], gate_b[:], ACT.Exp).then_inc(gb_done, 1)
                high_ahead(4)
                act.wait_ge(tile_done, tile(i, T_Q) + 1)
                nc.scalar.activation(cols2(qT[:], HALFO), psum2(0, HALFO), ACT.Copy, scale=HD ** -0.5).then_inc(q_kept, 1)
                act.wait_ge(tile_done, tile(i, T_CT) + 1)
                nc.scalar.activation(ckT[:], dense[:, 1, 0, 0:2 * P], ACT.Copy).then_inc(ckT_kept, 1)
                high_ahead(5)
                softplus_logs(2 * i)
                high_ahead(6)
                probabilities(2 * i)
                unturn(i, T_VT, 0, v_tok, vtok_kept)
                act.wait_ge(vtok_kept, i + 1)
                rows_out(v_tok, nvp, nvs, i)
                softplus_logs(2 * i + 1)
                high_ahead(7)
                log_sigmoid_parts(psum2(1, HALFO), gate_a[:], HALFO, tile(i, T_G) + 1, ga_abs, ga_exp, ga_ln, i + 1, None)
                act.wait_ge(ga_log, i + 1)
                nc.scalar.activation(gate_a[:], gate_a[:], ACT.Exp).then_inc(ga_done, 1)
                probabilities(2 * i + 1)
                unturn(i, T_KT, 0, k_tok, ktok_kept)
                act.wait_ge(ktok_kept, i + 1)
                rows_out(k_tok, nkp, nks, i)
                act.wait_ge(tile_done, tile(i, T_GT) + 1)
                nc.scalar.activation(glu_tok[:], dense[0:92, 1, 0, 0:P], ACT.Copy).then_inc(glutok_kept, 1)
                act.wait_ge(glutok_kept, i + 1)
                act.dma_start(ncp[:, bass.ds(i, 1), :].rearrange("t n c -> t (n c)"), glu_tok[0:PAD, :]).then_inc(kv_out, 16)
                act.dma_start(ncs[:, bass.ds(i, 1), :].rearrange("t n c -> t (n c)"), glu_tok[92 - PAD:92, :]).then_inc(kv_out, 16)
                act.wait_ge(kv_out, 16 * 8 * (i + 1))

            with act.Fori(0, KC) as i:
                turn(i)

            def high_post(g, n):
                high((n + 2) % RING, raw_post[(n + 2) % RING], 16 * (g + 1), FIRST_POST + 4 * g + n - 1)

            def post_group(g, body, last=False):
                for n in range(4):
                    if not (last and n >= 2):
                        high_post(g, n)
                    body(n)

            for k in range(KC):
                act.wait_ge(centred, k + 1)
                if k >= 2:
                    act.wait_ge(ssum_done, k - 1)
                nc.scalar.activation(part[:, k % 2, :], yconv[:, k, :], ACT.Square).then_inc(ysq_done, 1)

            def post(first, last, body, j0=0, final=False):
                with act.Fori(first, last) as g:
                    post_group(g, lambda n: body(g, 4 * (g - first) + n, n))

            def gate_conv(g, f, n):
                act.wait_ge(tile_done, FIRST_POST + 4 * g + n + 1)
                nc.scalar.activation(cols2(gate_c[:, bass.ds(f, 1), :].rearrange("p n c -> p (n c)"), HALFO), psum2(n % 2, HALFO), ACT.Sigmoid).then_inc(emptied[n % 2], 1)
            post(0, 2, gate_conv)
            inverse_root(var_done, 1, 2, OUTTOK, HALFO)
            for k in range(KC):
                act.wait_ge(u_done, k + 1)
                nc.scalar.activation(n32[:, k % 2, 0:OUTTOK], yconv[:, k, :], ACT.Silu, bias=vec(B_LN, k)).then_inc(silu_done, 1)
                act.wait_ge(silu_done, k + 1)
                nc.scalar.activation(s_hi[:, k, :], n32[:, k % 2, 0:OUTTOK], ACT.Copy).then_inc(nhi_done, 1)

            def merge(g, f, n):
                act.wait_ge(m_done, f + 1)
                nc.scalar.activation(r_hi[:, bass.ds(f, 1), 0:OUTTOK].rearrange("p n c -> p (n c)"), n32[:, n % 2, 0:OUTTOK], ACT.Copy).then_inc(mhi_done, 1)
            post(2, 4, merge)

            def out_squares(g, f, n):
                act.wait_ge(emptied[n % 2], emptied_at(g, n))
                nc.scalar.activation(n32[:, 0, 0:OUTTOK], xT[:, bass.ds(f, 1), META:].rearrange("p n c -> p (n c)"), ACT.Square).then_inc(x2sq_done, 1)
                act.wait_ge(x2sum_done, f + 1)
            post(4, 6, out_squares)
            inverse_root(ss2_done, 1, 3, OUTTOK, HALFO)
            for k in range(KC):
                split_high(k, OUTTOK, n32_done, KC + k + 1, r_hi[:, k, 0:OUTTOK], nhi_done)

            for rr in range(2):
                def up(g, f, n, half):
                    U = 2 * KC * rr + f
                    act.wait_ge(tile_done, FIRST_POST + 4 * g + n + 1)
                    nc.scalar.activation(cols2(n32[:, n % 2, 0:OUTTOK], HALFO), psum2(n % 2, HALFO), ACT.Relu).then_inc(emptied[n % 2], 1)
                    act.wait_ge(u32_done, U + 1)
                    nc.scalar.activation(u_hi[:, half, bass.ds(f - KC * half, 1), :].rearrange("p n c -> p (n c)"), n32[:, n % 2, 0:OUTTOK], ACT.Copy).then_inc(uhi_done, 1)
                for half in range(2):
                    g0 = 6 + 8 * rr
                    with act.Fori(g0 + 2 * half, g0 + 2 * half + 2) as g:
                        post_group(g, lambda n: up(g, 4 * (g - g0) + n, n, half))
                if rr == 0:
                    with act.Fori(10, 14) as g:
                        post_group(g, lambda n: None)
                else:
                    with act.Fori(18, 20) as g:
                        post_group(g, lambda n: None)
                    for g in (20, 21):
                        def down_squares(n):
                            f = 4 * (g - 20) + n
                            act.wait_ge(emptied[n % 2], emptied_at(g, n))
                            nc.scalar.activation(n32[:, 0, 0:OUTTOK], xT[:, f, META:], ACT.Square).then_inc(x2sq_done, 1)
                            act.wait_ge(x2sum_done, KC + f + 1)
                        post_group(g, down_squares, last=(g == 21))
            inverse_root(ss2_done, 2, 4, OUTTOK, HALFO)
            for t in range(1, 5, 2):
                n = P if t < 4 else DEC
                act.wait_ge(tile_done, FIRST_POST + 4 * N_GROUPS + t + 1)
                if t >= 2:
                    act.wait_ge(y_out[1], 16 * (t // 2))
                nc.scalar.activation(y_rows(1)[0:n].rearrange("p (h c) -> p h c", h=2), dense[0:n, 1, :, :], ACT.Copy).then_inc(ytok_kept[1], 1)
            act.wait_ge(kv_out, 16 * 8 * KC)

        @block.vector
        def _(dve):
            nc.vector.memset(eps_col[:], EPS).then_inc(eps_set, 1)
            dve.wait_ge(rows_turned, 1)
            nc.vector.tensor_copy(vecs[:], z[:, 1, 0:6 * KC]).then_inc(rows_kept, 1)
            for k in range(KC):
                dve.wait_ge(tile_done, k + 1)
                nc.vector.tensor_copy(xT[:, k, 0:512], dense[:, k % 2, 0, :])
                nc.vector.tensor_copy(xT[:, k, 512:TOK], dense[:, k % 2, 1, 0:TOK - 512]).then_inc(emptied[k % 2], 1)

            def normalise(g, c0, cols, base):
                ready = r_ready if g == G_MIX else h2_ready
                for k in range(KC + 1):
                    if k < KC:
                        if k >= 2:
                            dve.wait_ge(ready, k - 1)
                        nc.vector.scalar_tensor_tensor(n32[:, k % 2, 0:cols], xT[:, k, c0:c0 + cols], vec(g, k), rstd[:, 0:cols], ALU.mult, ALU.mult).then_inc(n32_done, 1)
                    if k >= 1:
                        dve.wait_ge(nhi_done, base + k)
                        nc.vector.tensor_tensor(r_lo[:, k - 1, 0:cols], n32[:, (k - 1) % 2, 0:cols], r_hi[:, k - 1, 0:cols].bitcast(F32), ALU.subtract)\
                            .then_inc(ready, 1)

            dve.wait_ge(rows_kept, 2)
            dve.wait_ge(emptied[1], KC // 2)
            dve.wait_ge(rstd_done, 1)
            normalise(G_MIX, 0, TOK, 0)
            dve.wait_ge(zeroed, 4)

            def turn(i):
                n = bass.ds(i, 1)
                y_cur = yconv[:, n, :].rearrange("p n c -> p (n c)")
                mixed_cur = mixed[:, n, :].rearrange("p n c -> p (n c)")
                taps = [0]

                def conv(count):
                    for _ in range(count):
                        k = taps[0]
                        taps[0] += 1
                        src, w, dst = conv_in[:, META + k:META + k + CONV_COLS], cw_cur[:, PAD + k:PAD + k + 1], acc[:, k % 2, :]
                        if k < 2:
                            nc.vector.tensor_scalar(dst, src, w, None, ALU.mult).then_inc(tap_done, 1)
                        else:
                            dve.wait_ge(tap_done, TAPS * i + k - 1)
                            nc.vector.scalar_tensor_tensor(dst, src, w, dst, ALU.mult, ALU.add).then_inc(tap_done, 1)

                def softplus_sum(head):
                    for b in range(3):
                        c = BANK_COLS[b]
                        dve.wait_ge(log_done, 3 * head + b + 1)
                        nc.vector.scalar_tensor_tensor(sp[:, b, 0:c], z[:, b, 0:c], 0.0, ez[:, b, 0:c], ALU.max, ALU.add).then_inc(sp_done, 1)

                def softplus_low(head):
                    for b in range(3):
                        c = BANK_COLS[b]
                        dve.wait_ge(sphi_done, 3 * head + b + 1)
                        nc.vector.tensor_tensor(sp_lo[:, b, 0:c], sp[:, b, 0:c], sp_hi[:, b, 0:c].bitcast(F32), ALU.subtract).then_inc(splo_done, 1)

                def keep_keys(t, slot, dst, kept):
                    dve.wait_ge(tile_done, tile(i, t) + 1)
                    nc.vector.tensor_copy(cols2(dst[:, 0:TOK], HALF), psum2(slot, HALF))
                    nc.vector.tensor_copy(dst[:, TOK:TOK + META], dense[:, slot, 0, 0:META]).then_inc(kept, 1)

                nc.vector.tensor_copy(cw_cur[:], cw[:, n, :].rearrange("p n c -> p (n c)"))
                nc.vector.tensor_copy(bdw_cur[:], vecs[:, bass.ds(B_DW * KC + i, 1)])
                nc.vector.tensor_copy(conv_in[:, CTX_CACHE:CTX_S], cw[:, n, 0:PAD].rearrange("p n c -> p (n c)")).then_inc(cur_done, 1)
                dve.wait_ge(gb_ln, i + 1)
                nc.vector.scalar_tensor_tensor(cols2(gate_b[:], HALF), psum2(1, HALF), 0.0, cols2(gate_b[:], HALF), ALU.min, ALU.subtract).then_inc(gb_log, 1)
                dve.wait_ge(gb_done, i + 1)
                nc.vector.tensor_tensor(conv_in[:, PAD:CTX_CACHE], a_sb[:, 0:META + SEQ], gate_b[:, 0:META + SEQ], ALU.mult)
                nc.vector.tensor_tensor(conv_in[:, CTX_S:], a_sb[:, META + SEQ:], gate_b[:, META + SEQ:], ALU.mult).then_inc(glu_done, 1)
                dve.wait_ge(glu_done, i + 1)
                dve.wait_ge(cur_done, i + 1)
                conv(6)
                keep_keys(T_K, 0, kT, k_kept)
                conv(5)
                softplus_sum(2 * i)
                conv(1)
                softplus_low(2 * i)
                keep_keys(T_V, 1, vT, v_kept)
                conv(8)
                conv(5)
                softplus_sum(2 * i + 1)
                conv(1)
                softplus_low(2 * i + 1)
                dve.wait_ge(ga_ln, i + 1)
                nc.vector.scalar_tensor_tensor(cols2(gate_a[:], HALFO), psum2(1, HALFO), 0.0, cols2(gate_a[:], HALFO), ALU.min, ALU.subtract).then_inc(ga_log, 1)
                conv(TAPS - taps[0])
                dve.wait_ge(ga_done, i + 1)
                dve.wait_ge(pv_done, 2 * (i + 1))
                nc.vector.tensor_tensor(mixed_cur[:, 0:SEQ], pv[:], gate_a[:, 0:SEQ], ALU.mult)
                nc.vector.tensor_tensor(mixed_cur[:, SEQ:], z[:, 1, S_PV:S_PV + DEC], gate_a[:, SEQ:], ALU.mult).then_inc(mix_done, 1)
                dve.wait_ge(tap_done, TAPS * (i + 1))
                nc.vector.scalar_tensor_tensor(y_cur[:, 0:SEQ], acc[:, 0, 0:SEQ], bdw_cur[:, 0:1], acc[:, 1, 0:SEQ], ALU.add, ALU.add)
                nc.vector.scalar_tensor_tensor(y_cur[:, SEQ:], acc[:, 0, CONV_COLS - DEC:], bdw_cur[:, 0:1], acc[:, 1, CONV_COLS - DEC:], ALU.add, ALU.add).then_inc(y_done, 1)
                dve.wait_ge(y_done, i + 1)
                nc.vector.tensor_tensor(sum_y[:], sum_y[:], y_cur, ALU.add).then_inc(sumy_done, 1)

            with dve.Fori(0, KC) as i:
                turn(i)

            dve.wait_ge(mean_done, 1)
            nc.vector.tensor_scalar(cols2(rstd[:, 0:OUTTOK], HALFO), z[:, 0:2, 0:HALFO], 1.0 / D, None, ALU.mult).then_inc(mean_kept, 1)
            dve.wait_ge(mean_kept, 1)
            nc.vector.memset(sum_sq[:], 0.0).then_inc(mean_kept, 1)
            dve.wait_ge(mean_kept, 2)
            for k in range(KC + 1):
                if k < KC:
                    nc.vector.tensor_tensor(yconv[:, k, :], yconv[:, k, :], rstd[:, 0:OUTTOK], ALU.subtract).then_inc(centred, 1)
                if k >= 1:
                    dve.wait_ge(ysq_done, k)
                    if k >= 2:
                        dve.wait_ge(ssum_done, k - 1)
                    nc.vector.tensor_tensor(sum_sq[:], sum_sq[:], part[:, (k - 1) % 2, :], ALU.add).then_inc(ssum_done, 1)
            dve.wait_ge(rstd_done, 2)
            for k in range(KC + 1):
                if k < KC:
                    nc.vector.scalar_tensor_tensor(yconv[:, k, :], yconv[:, k, :], vec(G_LN, k), rstd[:, 0:OUTTOK], ALU.mult, ALU.mult).then_inc(u_done, 1)
                if k >= 1:
                    dve.wait_ge(nhi_done, KC + k)
                    nc.vector.tensor_tensor(s_lo[:, k - 1, :], n32[:, (k - 1) % 2, 0:OUTTOK], s_hi[:, k - 1, :].bitcast(F32), ALU.subtract).then_inc(s_ready, 1)

            with dve.Fori(2, 4) as g:
                for n in range(4):
                    f = 4 * (g - 2) + n
                    fs = bass.ds(f, 1)
                    flat = "p n c -> p (n c)"
                    dve.wait_ge(tile_done, FIRST_POST + 4 * g + n + 1)
                    nc.vector.tensor_tensor(cols2(part[:, n % 2, :], HALFO), psum2(n % 2, HALFO), cols2(gate_c[:, fs, :].rearrange(flat), HALFO), ALU.mult)\
                        .then_inc(emptied[n % 2], 1)
                    dve.wait_ge(emptied[n % 2], emptied_at(g, n))
                    nc.vector.tensor_tensor(n32[:, n % 2, 0:OUTTOK], part[:, n % 2, :], mixed[:, fs, :].rearrange(flat), ALU.add).then_inc(m_done, 1)
                    dve.wait_ge(mhi_done, f + 1)
                    nc.vector.tensor_tensor(r_lo[:, fs, 0:OUTTOK].rearrange(flat), n32[:, n % 2, 0:OUTTOK], r_hi[:, fs, 0:OUTTOK].rearrange(flat).bitcast(F32), ALU.subtract)\
                        .then_inc(m_ready, 1)

            def residual(tile_n, slot, x_cur, count):
                dve.wait_ge(tile_done, tile_n)
                nc.vector.tensor_tensor(cols2(x_cur, HALFO), psum2(slot, HALFO), cols2(x_cur, HALFO), ALU.add).then_inc(emptied[slot], 1)

            def add_square(count):
                dve.wait_ge(x2sq_done, count)
                nc.vector.tensor_tensor(n32[:, 1, 0:OUTTOK], n32[:, 1, 0:OUTTOK], n32[:, 0, 0:OUTTOK], ALU.add).then_inc(x2sum_done, 1)

            dve.wait_ge(m_ready, KC)
            nc.vector.memset(n32[:, 1, :], 0.0).then_inc(mean_kept, 1)
            dve.wait_ge(mean_kept, 3)
            with dve.Fori(4, 6) as g:
                for n in range(4):
                    f = 4 * (g - 4) + n
                    residual(FIRST_POST + 4 * g + n + 1, n % 2, xT[:, bass.ds(f, 1), META:].rearrange("p n c -> p (n c)"), None)
                    add_square(f + 1)
            dve.wait_ge(rstd_done, 3)
            normalise(G_MLP, META, OUTTOK, 2 * KC)

            for rr in range(2):
                for half in range(2):
                    g0 = 6 + 8 * rr + 2 * half
                    with dve.Fori(g0, g0 + 2) as g:
                        for n in range(4):
                            f = 4 * (g - g0) + n
                            U = KC * (2 * rr + half) + f
                            dve.wait_ge(emptied[n % 2], emptied_at(g, n))
                            nc.vector.tensor_tensor(n32[:, n % 2, 0:OUTTOK], n32[:, n % 2, 0:OUTTOK], n32[:, n % 2, 0:OUTTOK], ALU.mult).then_inc(u32_done, 1)
                            dve.wait_ge(uhi_done, U + 1)
                            fs = bass.ds(f, 1)
                            nc.vector.tensor_tensor(u_lo[:, half, fs, :].rearrange("p n c -> p (n c)"), n32[:, n % 2, 0:OUTTOK],
                                                    u_hi[:, half, fs, :].rearrange("p n c -> p (n c)").bitcast(F32), ALU.subtract).then_inc(u_ready, 1)
                for half in range(2):
                    g0 = 10 + 8 * rr + 2 * half
                    if rr == 1 and half == 1:
                        dve.wait_ge(u_ready, 4 * KC)
                        nc.vector.memset(n32[:, 1, :], 0.0).then_inc(mean_kept, 1)
                        dve.wait_ge(mean_kept, 4)
                    with dve.Fori(g0, g0 + 2) as g:
                        for n in range(4):
                            f = 4 * (g - g0) + n
                            residual(FIRST_POST + 4 * g + n + 1, n % 2, xT[:, bass.ds(f, 1), META:].rearrange("p n c -> p (n c)"), None)
                            if rr == 1 and half == 1:
                                add_square(KC + f + 1)
            dve.wait_ge(rstd_done, 4)
            for k in range(KC):
                nc.vector.scalar_tensor_tensor(xT[:, k, META:], xT[:, k, META:], vec(G_FINAL, k), rstd[:, 0:OUTTOK], ALU.mult, ALU.mult).then_inc(fin_done, 1)
            for t in range(0, 5, 2):
                n = P if t < 4 else DEC
                dve.wait_ge(tile_done, FIRST_POST + 4 * N_GROUPS + t + 1)
                if t >= 2:
                    dve.wait_ge(y_out[0], 16 * (t // 2))
                nc.vector.tensor_copy(y_rows(0)[0:n].rearrange("p (h c) -> p h c", h=2), dense[0:n, 0, :, :]).then_inc(ytok_kept[0], 1)


_INS = ["x_prompt", "x_sample", "cache_k", "cache_v", "cache_conv", "meta", "g_mix", "w_in", "w_dw", "b_dw",
        "g_ln_conv", "b_ln_conv", "w_pw2", "w_out", "g_mlp", "w_up", "w_down", "g_final"]
_OUTS = [(1, SEQ, D), (1, DEC, D), (1, 1, META + SEQ, HEADS, HD), (1, 1, META + SEQ, HEADS, HD), (1, 1, PAD, D),
         (1, 1, DEC, HEADS, HD), (1, 1, DEC, HEADS, HD), (1, 1, PAD, D)]


def kernel(**inputs):
    import numpy as _np
    import concourse.bacc as _bacc
    from concourse.bass_utils import run_bass_kernel_spmd as _run

    nc = _bacc.Bacc("TRN2", target_bir_lowering=False, num_devices=1)
    arrays, args = {}, []
    for name in _INS:
        a = _np.ascontiguousarray(inputs[name])
        arrays[f"in_{name}_dram"] = a
        args.append(nc.dram_tensor(f"in_{name}_dram", a.shape, mybir.dt.from_np(a.dtype), kind="ExternalInput").ap())
    for n, shape in enumerate(_OUTS):
        args.append(nc.dram_tensor(f"out_{n}_dram", shape, F32, kind="ExternalOutput").ap())
    build(nc, *args)
    r = _run(nc, [arrays], core_ids=[0])
    return tuple(r.results[0][f"out_{n}_dram"] for n in range(len(_OUTS)))
```

```python
from contextlib import ExitStack

import concourse.bass as bass
from concourse import mybir

P = 128
ACT = mybir.ActivationFunctionType
ALU = mybir.AluOpType
F32 = mybir.dt.float32
F32R = mybir.dt.float32r
BF16 = mybir.dt.bfloat16

D = 1024
KC = D // P
HEADS, HD = 16, 64
META, SEQ, DEC = 16, 512, 32
PAST = 256
TAPS = 31
PAD = TAPS - 1
FF = 4 * D
EPS = 1e-6
TOK = META + SEQ + DEC
OUTTOK = SEQ + DEC
HALF, HALFO = TOK // 2, OUTTOK // 2
KEYS = 5 * P
NEG = -1e30

LOOP_UNITS = 6
N_LOOP = KC * LOOP_UNITS
RING_LOOP, RING = 3, 4
GROUPS_PER_STAGE = KC // 4
ROUNDS = 4
N_GROUPS = (3 + 2 * ROUNDS) * GROUPS_PER_STAGE

T_K, T_CT, T_V, T_A, T_VT, T_B, T_G, T_Q_NEXT, T_KT = range(1, 10)
LOOP_TILES = 9
FIRST_POST = KC + KC * LOOP_TILES

KT = [(0, 0, 512, 0), (1, 0, 400, 112), (2, 0, 272, 240), (2, 304, 144, 368)]
LAST, N_LAST = (1, 400), META + DEC
S_CACHE0, S_CACHE1, S_OWN = (2, 272), (2, 448), (1, 416)
BANKS = (0, 2, 1)
BANK_COLS = (512, 448, 480)
S_PV = 448


def build(nc, x_prompt, x_sample, cache_k, cache_v, cache_conv, meta, g_mix, w_in, w_dw, b_dw,
          g_ln_conv, b_ln_conv, w_pw2, w_out, g_mlp, w_up, w_down, g_final,
          y_prompt, y_sample, new_k_prompt, new_v_prompt, new_conv_prompt,
          new_k_sample, new_v_sample, new_conv_sample):
    xp, xs = x_prompt[0], x_sample[0]

    def weight(w, name):
        return w.rearrange("(k p) (n c) -> p k n c", p=P, c=P)

    win_v = weight(w_in[0], "in")
    wpw_v = weight(w_pw2[0], "pw2")
    wout_v = weight(w_out[0], "out")
    wup_v = weight(w_up[0], "up")
    wdown_v = w_down[0].rearrange("(r k p) (n c) -> p r k n c", p=P, k=KC, c=P)
    ck_v = cache_k[0, 0].rearrange("(t p) h d -> p t (h d)", p=P).rearrange("p t (n c) -> p t n c", c=P)
    cv_v = cache_v[0, 0].rearrange("(t p) h d -> p t (h d)", p=P).rearrange("p t (n c) -> p t n c", c=P)

    def rows(o):
        return o[0, 0].rearrange("t h d -> t (h d)").rearrange("t (n c) -> t n c", c=P)

    nkp, nvp, nks, nvs = rows(new_k_prompt), rows(new_v_prompt), rows(new_k_sample), rows(new_v_sample)
    ncp = new_conv_prompt[0, 0].rearrange("t (n c) -> t n c", c=P)
    ncs = new_conv_sample[0, 0].rearrange("t (n c) -> t n c", c=P)

    with ExitStack() as ctx:
        def sb(name, shape, dt=F32, where=ctx):
            return where.enter_context(nc.sbuf_tensor(name, shape, dt))

        def sem(name):
            return ctx.enter_context(nc.semaphore(name))

        w_raw = sb("w_raw", [P, RING, KC, P])
        w_hi = sb("w_hi", [P, RING, KC, P], F32R)
        w_lo = sb("w_lo", [P, RING, KC, P], F32R)
        xT = sb("xT", [P, KC, TOK])
        r_hi = sb("r_hi", [P, KC, TOK], F32R)
        r_lo = sb("r_lo", [P, KC, TOK], F32R)
        ident = sb("ident", [P, P])
        ident_b = sb("ident_b", [P, P], BF16)
        ones = sb("ones", [P, P])
        tri = sb("tri", [P, P], F32R)
        negones = sb("negones", [P, P], F32R)
        own_all = sb("own_all", [P, P], F32R)
        own_own = sb("own_own", [P, P], F32R)
        cache_meta = sb("cache_meta", [P, P], F32R)
        neg_diag = sb("neg_diag", [P, P], BF16)
        neg_last = sb("neg_last", [P, N_LAST], BF16)
        cw = sb("cw", [P, KC, PAD + TAPS])
        vecs = sb("vecs", [P, 6 * KC])
        eps_col = sb("eps_col", [P, 1])
        rstd_tok = sb("rstd_tok", [P, 5])
        rstd = sb("rstd", [P, TOK])
        n32 = sb("n32", [P, 2, TOK])

        sq = n32

        def vec(n, k):
            return vecs[:, n * KC + k:n * KC + k + 1]
        G_MIX, B_DW, G_LN, B_LN, G_MLP, G_FINAL = range(6)

        late = ExitStack()
        u_hi = sb("u_hi", [P, KC, OUTTOK], F32R, where=late)
        u_lo = sb("u_lo", [P, KC, OUTTOK], F32R, where=late)
        late.close()
        mid = ExitStack()
        yconv = sb("yconv", [P, KC, OUTTOK], where=mid)
        mixed = sb("mixed", [P, KC, OUTTOK], where=mid)
        sum_y = sb("sum_y", [P, OUTTOK], where=mid)

        loop = ExitStack()
        vT = sb("vT", [P, KEYS], where=loop)
        ck_tok = sb("ck_tok", [P, 2, P], where=loop)
        start = ExitStack()
        x_tok = sb("x_tok", [P, 5, D], where=start)
        cw_rows = sb("cw_rows", [PAD + TAPS, D], where=start)
        vec_rows = sb("vec_rows", [6 * KC, P], where=start)
        mat_f = sb("mat_f", [P, 5, P], where=start)
        start.close()
        qT = sb("qT", [P, OUTTOK], where=loop)
        ckT = sb("ckT", [P, 2 * P], where=loop)
        a_sb = sb("a_sb", [P, TOK], where=loop)
        gate_b = sb("gate_b", [P, TOK], where=loop)
        sp = sb("sp", [P, 3, 512], where=loop)
        ez = sb("ez", [P, 3, 512], where=loop)
        sp_hi = sb("sp_hi", [P, 3, 512], F32R, where=loop)
        sp_lo = sb("sp_lo", [P, 3, 512], F32R, where=loop)
        prob = ez
        kT = sb("kT", [P, KEYS], where=loop)
        v_tok = sb("v_tok", [P, 5, P], where=loop)
        k_tok = sb("k_tok", [P, 5, P], where=loop)
        glu_tok = sb("glu_tok", [92, P], where=loop)
        cv_tok = sb("cv_tok", [P, 2, P], where=loop)
        CTX_CACHE = PAD + META + SEQ
        CTX_S = CTX_CACHE + PAD
        CONV_COLS = CTX_S + DEC - META - PAD
        conv_in = sb("conv_in", [P, CTX_S + DEC], where=loop)
        acc = sb("acc", [P, 2, CONV_COLS], where=loop)
        cw_cur = sb("cw_cur", [P, PAD + TAPS], where=loop)
        bdw_cur = sb("bdw_cur", [P, 1], where=loop)
        gate_a = sb("gate_a", [P, OUTTOK], where=loop)
        loop.close()

        post = ExitStack()
        gate_c = sb("gate_c", [P, KC, OUTTOK], where=post)
        part = sb("part", [P, 2, OUTTOK], where=post)
        sum_sq = sb("sum_sq", [P, OUTTOK], where=post)
        rows_back = ExitStack()
        y_tok = sb("y_tok", [P, 5, D], where=rows_back)
        rows_back.close()
        s_hi = sb("s_hi", [P, KC, OUTTOK], F32R, where=post)
        s_lo = sb("s_lo", [P, KC, OUTTOK], F32R, where=post)
        post.close()
        mid.close()

        dense = ctx.enter_context(nc.psum_tensor("dense", [P, 2, 2, 512], F32))
        z = ctx.enter_context(nc.psum_tensor("z", [P, 3, 512], F32))
        pv = ctx.enter_context(nc.psum_tensor("pv", [P, 512], F32))

        x_loaded = sem("x_loaded")
        rows_loaded = sem("rows_loaded")
        raw_loop = [sem(f"raw_loop{n}") for n in range(LOOP_UNITS)]
        raw_post = [sem(f"raw_post{n}") for n in range(4)]
        ck_loaded, cv_loaded = sem("ck_loaded"), sem("cv_loaded")
        hi_done, lo_done = sem("hi_done"), sem("lo_done")
        tile_done = sem("tile_done")
        emptied = [sem("emptied0"), sem("emptied1")]
        consts, mats = sem("consts"), sem("mats")
        rows_turned, rows_kept = sem("rows_turned"), sem("rows_kept")
        sq_done, ss_done = sem("sq_done"), sem("ss_done")
        eps_set, mean_kept = sem("eps_set"), sem("mean_kept")
        ln_step, rstd_done = sem("ln_step"), sem("rstd_done")
        n32_done, nhi_done, r_ready = sem("n32_done"), sem("nhi_done"), sem("r_ready")
        cur_done = sem("cur_done")
        a_kept, gb_abs, gb_exp, gb_ln, gb_log, gb_done = (sem(n) for n in ("a_kept", "gb_abs", "gb_exp", "gb_ln", "gb_log", "gb_done"))
        ga_abs, ga_exp, ga_ln, ga_log, ga_done = (sem(n) for n in ("ga_abs", "ga_exp", "ga_ln", "ga_log", "ga_done"))
        glu_done, tap_done, y_done = sem("glu_done"), sem("tap_done"), sem("y_done")
        q_kept, ckT_kept, k_kept, v_kept = sem("q_kept"), sem("ckT_kept"), sem("k_kept"), sem("v_kept")
        vtok_kept, ktok_kept, glutok_kept = sem("vtok_kept"), sem("ktok_kept"), sem("glutok_kept")
        z_scored, abs_done, exp_done, log_done = sem("z_scored"), sem("abs_done"), sem("exp_done"), sem("log_done")
        sp_done, sphi_done, splo_done = sem("sp_done"), sem("sphi_done"), sem("splo_done")
        cum_done, prob_done, pv_done = sem("cum_done"), sem("prob_done"), sem("pv_done")
        mix_s_done, mix_done, gates_done = sem("mix_s_done"), sem("mix_done"), sem("gates_done")
        kv_out = sem("kv_out")
        sumy_done, mean_done, centred, ysq_done, ssum_done = (sem(n) for n in ("sumy_done", "mean_done", "centred", "ysq_done", "ssum_done"))
        var_done, u_done, silu_done, s_ready = (sem(n) for n in ("var_done", "u_done", "silu_done", "s_ready"))
        m_done, mhi_done, m_ready = (sem(n) for n in ("m_done", "mhi_done", "m_ready"))
        x2sq_done, x2sum_done, ss2_done = (sem(n) for n in ("x2sq_done", "x2sum_done", "ss2_done"))
        h2_ready, u32_done, uhi_done, u_ready = (sem(n) for n in ("h2_ready", "u32_done", "uhi_done", "u_ready"))
        fin_done = sem("fin_done")
        xg_done, turned, half_kept = sem("xg_done"), sem("turned"), sem("half_kept")
        y_by_dve, y_by_act, y_out = sem("y_by_dve"), sem("y_by_act"), sem("y_out")
        zeroed = sem("zeroed")

        def tile(i, t):
            return KC + LOOP_TILES * i + t

        UNIT_TILE = (T_Q_NEXT - LOOP_TILES, T_K, T_V, T_A, T_B, T_G)

        def emptied_at(g, n):
            return KC // 2 + 2 * g + n // 2 + 1

        def psum2(slot, half):
            return dense[:, slot, :, 0:half]

        def cols2(ap, half):
            return ap.rearrange("p (h c) -> p h c", c=half)

        block = ctx.enter_context(nc.Block())

        @block.sync
        def _(sync):
            for dst, src in ((x_tok[0:META, 0, :], meta), (x_tok[META:P, 0, :], xp[0:P - META]),
                             (x_tok[:, 1:4, :], xp[P - META:4 * P - META].rearrange("(t p) d -> p t d", p=P)),
                             (x_tok[0:META, 4, :], xp[4 * P - META:SEQ]), (x_tok[META:META + DEC, 4, :], xs)):
                sync.dma_start(dst, src).then_inc(x_loaded, 16)
            for n, v in enumerate((g_mix, b_dw, g_ln_conv, b_ln_conv, g_mlp)):
                sync.dma_start(vec_rows[n * KC:(n + 1) * KC, :], v[0].rearrange("(k p) -> k p", p=P)).then_inc(rows_loaded, 16)
            sync.dma_start(vec_rows[5 * KC:, :], g_final.rearrange("(k p) -> k p", p=P)).then_inc(rows_loaded, 16)
            sync.dma_start(cw_rows[0:PAD, :], cache_conv[0, 0]).then_inc(rows_loaded, 16)
            sync.dma_start(cw_rows[PAD:, :], w_dw[0]).then_inc(rows_loaded, 16)

            BASE = [2 * KC, 3 * KC, 4 * KC, 0, KC, 6 * KC]

            def loads(i, first):
                for u in range(LOOP_UNITS):
                    if not (first and u < RING_LOOP):
                        sync.wait_ge(lo_done, LOOP_UNITS * i + u - 2)
                    sync.dma_start(w_raw[:, u % RING_LOOP], win_v[:, :, bass.ds(BASE[u] + i, 1), :].rearrange("p k n c -> p k (n c)")).then_inc(raw_loop[u], 16)
                    if u == 0:
                        if not first:
                            sync.wait_ge(ckT_kept, i)
                        sync.dma_start(ck_tok[:], ck_v[:, :, bass.ds(i, 1), :].rearrange("p t n c -> p t (n c)")).then_inc(ck_loaded, 16)
                    if u == 5:
                        if not first:
                            sync.wait_ge(pv_done, 2 * i)
                        sync.dma_start(cv_tok[:], cv_v[:, :, bass.ds(i, 1), :].rearrange("p t n c -> p t (n c)")).then_inc(cv_loaded, 16)

            loads(0, True)
            with sync.Fori(1, KC) as i:
                loads(i, False)

            for n in range(4):
                sync.wait_ge(lo_done, N_LOOP + n - 2)
                sync.dma_start(w_raw[:, n], win_v[:, :, 5 * KC + n, :]).then_inc(raw_loop[n] if n < 2 else raw_post[n], 16)

            def load_group(g, view):
                for n in range(4):
                    sync.wait_ge(lo_done, N_LOOP + 4 * g + n - 3)
                    sync.dma_start(w_raw[:, n], view(n)).then_inc(raw_post[n], 16)

            load_group(1, lambda n: win_v[:, :, 5 * KC + 4 + n, :])
            for first_group, view in ((2, wpw_v), (4, wout_v)):
                with sync.Fori(0, 2) as j:
                    load_group(first_group + j, lambda n: view[:, :, bass.ds(4 * j + n, 1), :].rearrange("p k n c -> p k (n c)"))
            with sync.Fori(0, 2) as rr:
                with sync.Fori(0, 4) as j:
                    load_group(6 + 8 * rr + j, lambda n: wup_v[:, :, bass.ds(16 * rr + 4 * j + n, 1), :].rearrange("p k n c -> p k (n c)"))
                for half in range(2):
                    with sync.Fori(0, 2) as j:
                        load_group(10 + 2 * half + 8 * rr + j, lambda n: wdown_v[:, bass.ds(2 * rr + half, 1), :, bass.ds(4 * j + n, 1), :].rearrange("p r k n c -> p (r k) (n c)"))

            for t, done, count in ((0, y_by_dve, 2), (2, y_by_act, 2), (1, y_by_dve, 4), (3, y_by_act, 4)):
                sync.wait_ge(done, count)
                sync.dma_start(y_prompt[0, t * P:(t + 1) * P, :], y_tok[:, t, :]).then_inc(y_out, 16)
            sync.wait_ge(y_by_dve, 5)
            sync.wait_ge(y_by_act, 5)
            sync.dma_start(y_sample[0], y_tok[0:DEC, 4, :]).then_inc(y_out, 16)
            sync.wait_ge(y_out, 16 * 5)

        @block.gpsimd
        def _(pool):
            pool.memset(ident[:], 0.0).then_inc(consts, 1)
            pool.memset(ones[:], 1.0).then_inc(consts, 1)
            pool.memset(neg_diag[:], 0.0).then_inc(consts, 1)
            pool.memset(neg_last[:], 0.0).then_inc(consts, 1)
            pool.memset(mat_f[:], -1.0).then_inc(consts, 1)
            pool.memset(kT[:, TOK + META:KEYS], 0.0).then_inc(zeroed, 1)
            pool.memset(vT[:, TOK + META:KEYS], 0.0).then_inc(zeroed, 1)
            pool.memset(conv_in[:, 0:PAD], 0.0).then_inc(zeroed, 1)
            pool.memset(sum_y[:], 0.0).then_inc(zeroed, 1)
            done = 5

            def select(ap, pattern, base, mult, fill, op=ALU.is_ge):
                nonlocal done
                pool.wait_ge(consts, done)
                pool.affine_select(out=ap, in_=ap, pattern=pattern, compare_op=op, fill=fill, base=base, channel_multiplier=mult).then_inc(consts, 1)
                done += 1

            select(ident[:], [[-1, P]], 0, 1, 1.0, ALU.not_equal)
            select(neg_diag[:], [[1, P]], -1, -1, NEG)
            select(neg_last[:, 0:META], [[1, META]], -1, -1, NEG)
            neg_own = neg_last[:, META:]
            select(neg_own, [[1, DEC]], META - 1, -1, NEG)
            select(neg_own, [[0, DEC]], META + DEC - 1, -1, 0.0)
            select(neg_own, [[0, DEC]], META + DEC + META - 1, -1, NEG)
            select(neg_own, [[0, DEC]], -META, 1, NEG)
            M0 = META + DEC
            select(mat_f[:, 0, :], [[-1, P]], 0, 1, 0.0)
            select(mat_f[:, 2, :], [[0, P]], M0 - 1, -1, 0.0)
            select(mat_f[:, 3, 0:M0], [[-1, M0]], 0, 1, 0.0)
            select(mat_f[:, 3, 0:M0], [[0, M0]], M0 - 1, -1, 0.0)
            select(mat_f[:, 3, M0:P], [[0, P - M0]], M0 - 1, -1, 0.0)
            select(mat_f[:, 3, M0:P], [[1, P - M0]], M0 - 1, -1, -1.0)
            select(mat_f[:, 4, :], [[1, P]], -M0, 0, 0.0)
            pool.wait_ge(consts, done)
            pool.tensor_copy(ident_b[:], ident[:]).then_inc(mats, 1)
            for n, m in enumerate((tri, negones, own_all, own_own, cache_meta)):
                pool.tensor_copy(m[:], mat_f[:, n, :]).then_inc(mats, 1)

            def low(u, s):
                pool.wait_ge(hi_done, u + 1)
                pool.tensor_tensor(w_lo[:, s], w_raw[:, s], w_hi[:, s].bitcast(F32), ALU.subtract).then_inc(lo_done, 1)

            with pool.Fori(0, N_LOOP // RING_LOOP) as j:
                for s in range(RING_LOOP):
                    low(RING_LOOP * j + s, s)
            with pool.Fori(0, N_GROUPS) as g:
                for s in range(RING):
                    low(N_LOOP + RING * g + s, s)

        @block.tensor
        def _(pe):
            def claim(slot, n):
                pe.wait_ge(emptied[slot], n)

            def dense_unit(wslot, slot, m_hi, m_lo, c0, half, chunk_ready=None):
                for k in range(KC):
                    if chunk_ready is not None:
                        pe.wait_ge(chunk_ready[0], chunk_ready[1] + k)
                    for n, (w, m) in enumerate(((w_hi, m_hi), (w_hi, m_lo), (w_lo, m_hi))):
                        for h in range(2):
                            mm = nc.tensor.matmul(dense[:, slot, h, 0:half], w[:, wslot, k, :], m[:, k, c0 + h * half:c0 + (h + 1) * half],
                                                  start=(k == 0 and n == 0), stop=(k == KC - 1 and n == 2))
                mm.then_inc(tile_done, 1)

            pe.wait_ge(consts, 19)
            pe.wait_ge(rows_loaded, 16 * 8)
            for k in range(KC):
                nc.tensor.transpose(z[:, 0, k * 61:(k + 1) * 61], cw_rows[:, k * P:(k + 1) * P], ident[0:61, 0:61])
            nc.tensor.transpose(z[:, 1, 0:6 * KC], vec_rows[:], ident[0:6 * KC, 0:6 * KC]).then_inc(rows_turned, 1)
            pe.wait_ge(x_loaded, 16 * 5)

            def x_squares(k):
                pe.wait_ge(sq_done, k + 1)
                for h in range(2):
                    mm = nc.tensor.matmul(z[:, h, 0:HALF], ones[:], sq[:, k % 2, h * HALF:(h + 1) * HALF], start=(k == 0), stop=(k == KC - 1))
                mm.then_inc(ss_done, 1)

            for k in range(KC):
                if k >= 2:
                    claim(k % 2, k // 2)
                for t in range(5):
                    n = P if t < 4 else META + DEC
                    mm = nc.tensor.transpose(dense[:, k % 2, t // 4, (t % 4) * P:(t % 4) * P + n], x_tok[0:n, t, k * P:(k + 1) * P], ident[0:n, 0:n])
                mm.then_inc(tile_done, 1)
                if k >= 1:
                    if k == 1:
                        pe.wait_ge(rows_kept, 2)
                    x_squares(k - 1)
            x_squares(KC - 1)
            pe.wait_ge(mats, 6)

            def scores(i, hh, first=False):
                r = slice(hh * HD, (hh + 1) * HD)
                if hh == 0:
                    pe.wait_ge(q_kept, i + 1)
                    pe.wait_ge(k_kept, i + 1)
                    pe.wait_ge(ckT_kept, i + 1)

                def score(bank, off, keys, q0, q1, start=False):
                    return nc.tensor.matmul(z[:, bank, off:off + q1 - q0], keys, qT[r, q0:q1], start=start, stop=False, skip_group_check=True)

                def mask(bank, off, m):
                    return nc.tensor.matmul(z[:, bank, off:off + m.shape[1]], ident_b[:], m, start=False, stop=False, skip_group_check=True)

                score(0, 0, kT[r, 0:P], 0, SEQ, start=True)
                mask(0, 0, neg_diag[:, META:P]).then_inc(z_scored, 1)
                for j in (2, 3):
                    bank, off, _, q0 = KT[j]
                    score(bank, off, kT[r, j * P:(j + 1) * P], q0, SEQ, start=(j == 2))
                    mask(bank, off, neg_diag[:])
                score(*S_CACHE0, ckT[r, 0:P], SEQ, OUTTOK)
                score(*S_CACHE1, ckT[r, P:2 * P], SEQ, OUTTOK).then_inc(z_scored, 1)
                if hh == 0 and not first:
                    pe.wait_ge(mix_s_done, i)
                bank, off, _, q0 = KT[1]
                score(bank, off, kT[r, P:2 * P], q0, SEQ, start=True)
                mask(bank, off, neg_diag[:])
                score(*LAST, kT[r, 4 * P:5 * P], SEQ - META, OUTTOK)
                mask(*LAST, neg_last[:]).then_inc(z_scored, 1)

            def cumulate(head):
                pe.wait_ge(splo_done, 3 * head + 3)

                def add(m, dst, n, src):
                    for part_ in (sp_hi, sp_lo):
                        mm = nc.tensor.matmul(z[:, dst[0], dst[1]:dst[1] + n], m[:], part_[:, src[0], src[1]:src[1] + n], start=False, stop=False, skip_group_check=True)
                    return mm
                b0, b1 = BANK_COLS[0], KT[1][2]
                add(tri, (0, 0), b0, (0, 0))
                add(tri, (2, 0), BANK_COLS[2], (2, 0))
                add(tri, (1, 0), b1, (1, 0))
                add(own_own, LAST, N_LAST, LAST)
                n3 = KT[3][2]
                add(negones, (2, KT[2][2] - n3), n3 + DEC, KT[3])
                for n, src in ((n3, KT[3]), (KT[2][2], KT[2])):
                    add(negones, (1, b1 - n), n, src)
                    add(negones, (0, b0 - n), n, src)
                add(negones, (0, b0 - b1), b1, KT[1])
                for cache in (S_CACHE0, S_CACHE1):
                    add(own_all, (2, cache[1] - META), N_LAST, LAST)
                add(negones, (1, b1 - META), META, LAST)
                add(negones, (0, b0 - META), META, LAST)
                add(cache_meta, S_OWN, DEC, S_CACHE0)
                add(cache_meta, S_OWN, DEC, S_CACHE1).then_inc(cum_done, 1)

            def values(i, hh, first=False):
                r = slice(hh * HD, (hh + 1) * HD)
                head = 2 * i + hh
                if hh == 0:
                    pe.wait_ge(vtok_kept, i + 1)
                    pe.wait_ge(cv_loaded, 16 * (i + 1))
                    if not first:
                        pe.wait_ge(mix_done, i)
                pe.wait_ge(prob_done, 3 * head + 3)
                for n, (bank, off, cols, q0) in enumerate(KT):
                    nc.tensor.matmul(pv[r, q0:SEQ], v_tok[:, n, r], prob[:, bank, off:off + cols], start=(n == 0), stop=False, skip_group_check=True)
                nc.tensor.matmul(pv[r, SEQ - META:SEQ], v_tok[:, 4, r], prob[:, LAST[0], LAST[1]:LAST[1] + META], start=False, stop=True, skip_group_check=True)
                for n, ((bank, off), v) in enumerate(((S_CACHE0, cv_tok[:, 0, r]), (S_CACHE1, cv_tok[:, 1, r]), (S_OWN, v_tok[:, 4, r]))):
                    mm = nc.tensor.matmul(z[r, 1, S_PV:S_PV + DEC], v, prob[:, bank, off:off + DEC], start=(n == 0), stop=(n == 2), skip_group_check=True)
                mm.then_inc(pv_done, 1)

            def turn_back(src, slot):
                for t in range(5):
                    mm = nc.tensor.transpose(dense[:, slot, t // 4, (t % 4) * P:(t % 4 + 1) * P], src[:, t * P:(t + 1) * P], ident[:])
                return mm

            def keys_back(i):
                pe.wait_ge(ga_log, i + 1)
                pe.wait_ge(glu_done, i + 1)
                turn_back(kT, 1)
                nc.tensor.transpose(dense[0:92, 1, 1, P:2 * P], conv_in[:, CTX_CACHE - PAD:CTX_S + DEC], ident[:]).then_inc(tile_done, 1)

            def turn(i, prev=None):
                first = prev is None
                def unit(u, slot, out_only=False, chunks=None):
                    pe.wait_ge(lo_done, LOOP_UNITS * i + u + 1)
                    dense_unit(u % RING_LOOP, slot, r_hi, r_lo, META if out_only else 0, HALFO if out_only else HALF, chunks)

                if first:
                    claim(0, KC // 2)
                    unit(0, 0, True, (r_ready, 1))
                    claim(1, KC // 2)
                else:
                    pe.wait_ge(gb_log, i)
                    unit(0, 0, True)
                    keys_back(prev)
                    cumulate(2 * i - 1)
                    pe.wait_ge(ktok_kept, i)
                unit(1, 1)
                pe.wait_ge(q_kept, i + 1)
                pe.wait_ge(ck_loaded, 16 * (i + 1))
                for t in range(2):
                    mm = nc.tensor.transpose(dense[:, 0, 0, t * P:(t + 1) * P], ck_tok[:, t, :], ident[:])
                mm.then_inc(tile_done, 1)
                if not first:
                    values(prev, 1)
                scores(i, 0, first)
                pe.wait_ge(k_kept, i + 1)
                unit(2, 1)
                pe.wait_ge(ckT_kept, i + 1)
                unit(3, 0)
                cumulate(2 * i)
                pe.wait_ge(v_kept, i + 1)
                turn_back(vT, 1).then_inc(tile_done, 1)
                pe.wait_ge(a_kept, i + 1)
                unit(4, 0)
                values(i, 0, first)
                scores(i, 1)
                pe.wait_ge(vtok_kept, i + 1)
                unit(5, 1, True)

            turn(0)
            with pe.Fori(0, KC - 1) as before:
                turn(before + 1, before)

            def unit(g, n, m_hi, m_lo, ready=None):
                pe.wait_ge(lo_done, N_LOOP + 4 * g + n + 1)
                claim(n % 2, KC // 2 + 2 * g + n // 2)
                dense_unit(n, n % 2, m_hi, m_lo, 0, HALFO, ready)

            def group(g, m_hi, m_lo, ready=None):
                for n in range(4):
                    unit(g, n, m_hi, m_lo, ready)

            def gate_conv(f):
                pe.wait_ge(lo_done, N_LOOP + f + 1)
                if f >= 2:
                    claim(f % 2, KC // 2 + f // 2)
                dense_unit(f % RING, f % 2, r_hi, r_lo, META, HALFO)

            pe.wait_ge(gb_log, KC)
            gate_conv(0)
            keys_back(KC - 1)
            cumulate(2 * KC - 1)
            pe.wait_ge(ktok_kept, KC)
            gate_conv(1)
            values(KC - 1, 1)
            gate_conv(2)
            gate_conv(3)
            pe.wait_ge(sumy_done, KC)
            for h in range(2):
                mm = nc.tensor.matmul(z[:, h, 0:HALFO], ones[:], sum_y[:, h * HALFO:(h + 1) * HALFO], start=True, stop=True)
            mm.then_inc(mean_done, 1)
            for f in (4, 5):
                gate_conv(f)
            pe.wait_ge(ssum_done, KC)
            for h in range(2):
                mm = nc.tensor.matmul(z[:, h, 0:HALFO], ones[:], sum_sq[:, h * HALFO:(h + 1) * HALFO], start=True, stop=True)
            mm.then_inc(var_done, 1)
            for f in (6, 7):
                gate_conv(f)
            with pe.Fori(2, 4) as g:
                group(g, s_hi, s_lo, (s_ready, 1))
            with pe.Fori(4, 6) as g:
                group(g, r_hi, r_lo, (m_ready, 1))

            u_parts = ((r_hi, r_lo), (u_hi, u_lo))
            unit(6, 0, s_hi, s_lo, (h2_ready, 1))
            pe.wait_ge(x2sum_done, KC)
            for h in range(2):
                mm = nc.tensor.matmul(z[:, h, 0:HALFO], ones[:], n32[:, 1, h * HALFO:(h + 1) * HALFO], start=True, stop=True)
            mm.then_inc(ss2_done, 1)
            for n in range(1, 4):
                unit(6, n, s_hi, s_lo)

            def tokens_back(f):
                pe.wait_ge(xg_done, f + 1)
                if f == 4:
                    pe.wait_ge(half_kept, 4)
                for t in range(4):
                    dst = pv if t == 3 else z[:, t]
                    mm = nc.tensor.transpose(dst[:, (f % 4) * P:(f % 4 + 1) * P], xT[:, f, META + t * P:META + (t + 1) * P], ident[:])
                mm.then_inc(turned, 1)

            def sample_back(f):
                pe.wait_ge(xg_done, f + 1)
                return nc.tensor.transpose(dense[0:DEC, 0, f // 4, (f % 4) * P:(f % 4 + 1) * P], xT[:, f, META + SEQ:], ident[:])

            for rr in range(2):
                with pe.Fori(7 if rr == 0 else 14, 10 + 8 * rr) as g:
                    group(g, s_hi, s_lo)
                with pe.Fori(10 + 8 * rr, 12 + 8 * rr) as g:
                    group(g, *u_parts[0], (u_ready, 16 * rr + 1))
                if rr == 0:
                    with pe.Fori(12, 14) as g:
                        group(g, *u_parts[1], (u_ready, KC + 1))
                else:
                    for f in range(KC):
                        unit(20 + f // 4, f % 4, *u_parts[1], (u_ready, 3 * KC + 1) if f == 0 else None)
                        if f >= 1:
                            tokens_back(f - 1)
            claim(0, KC // 2 + 2 * N_GROUPS)
            for f in range(KC - 1):
                sample_back(f)
            tokens_back(KC - 1)
            sample_back(KC - 1).then_inc(turned, 1)
            claim(1, KC // 2 + 2 * N_GROUPS)
            pe.wait_ge(x2sum_done, 2 * KC)
            for t in range(5):
                n = P if t < 4 else DEC
                mm = nc.tensor.matmul(dense[0:n, 1, 0, t:t + 1], n32[:, 1, t * P:t * P + n], ones[:, 0:1], start=(t == 0), stop=True, skip_group_check=True)
            mm.then_inc(ss2_done, 1)

        @block.scalar
        def _(act):
            def high(s, raw_sem, raw_count, free_tile):
                act.wait_ge(raw_sem, raw_count)
                if free_tile is not None:
                    act.wait_ge(tile_done, free_tile)
                nc.scalar.activation(w_hi[:, s], w_raw[:, s], ACT.Copy).then_inc(hi_done, 1)

            act.preload_act_table_set("natural_log_exp_and_others")
            act.wait_ge(rows_turned, 1)
            nc.scalar.activation(cw[:].rearrange("p k r -> p (k r)"), z[:, 0, 0:KC * 61], ACT.Copy).then_inc(rows_kept, 1)
            for k in range(KC):
                act.wait_ge(emptied[k % 2], k // 2 + 1)
                if k >= 2:
                    act.wait_ge(ss_done, k - 1)
                nc.scalar.activation(sq[:, k % 2, :], xT[:, k, :], ACT.Square).then_inc(sq_done, 1)
            high(0, raw_loop[0], 16, None)
            high(1, raw_loop[1], 16, None)

            def inverse_root(psum_sem, count, step, cols, half):
                act.wait_ge(psum_sem, count)
                nc.scalar.activation(cols2(rstd[:, 0:cols], half), z[:, 0:2, 0:half], ACT.Ln, scale=1.0 / D, bias=eps_col[:, 0:1]).then_inc(ln_step, 1)
                act.wait_ge(ln_step, step)
                nc.scalar.activation(rstd[:, 0:cols], rstd[:, 0:cols], ACT.Exp, scale=-0.5).then_inc(rstd_done, 1)

            def split_high(n, cols, ready, ready_count, dst, done):
                act.wait_ge(ready, ready_count)
                nc.scalar.activation(dst, n32[:, n % 2, 0:cols], ACT.Copy).then_inc(done, 1)

            act.wait_ge(eps_set, 1)
            inverse_root(ss_done, KC, 1, TOK, HALF)
            for k in range(KC):
                split_high(k, TOK, n32_done, k + 1, r_hi[:, k, :], nhi_done)

            def log_sigmoid_parts(src, dst, half, tile_n, s_abs, s_exp, s_ln, count):
                act.wait_ge(tile_done, tile_n)
                nc.scalar.activation(cols2(dst, half), src, ACT.Abs).then_inc(s_abs, 1)
                act.wait_ge(s_abs, count)
                nc.scalar.activation(dst, dst, ACT.Exp, scale=-1.0).then_inc(s_exp, 1)
                act.wait_ge(s_exp, count)
                nc.scalar.activation(dst, dst, ACT.Ln, bias=1.0).then_inc(s_ln, 1)

            def softplus_logs(head):
                def a(n):
                    b, c = BANKS[n], BANK_COLS[BANKS[n]]
                    act.wait_ge(z_scored, 3 * head + n + 1)
                    nc.scalar.activation(ez[:, b, 0:c], z[:, b, 0:c], ACT.Abs).then_inc(abs_done, 1)

                def e(n):
                    b, c = BANKS[n], BANK_COLS[BANKS[n]]
                    act.wait_ge(abs_done, 3 * head + n + 1)
                    nc.scalar.activation(ez[:, b, 0:c], ez[:, b, 0:c], ACT.Exp, scale=-1.0).then_inc(exp_done, 1)

                def l(n):
                    b, c = BANKS[n], BANK_COLS[BANKS[n]]
                    act.wait_ge(exp_done, 3 * head + n + 1)
                    nc.scalar.activation(ez[:, b, 0:c], ez[:, b, 0:c], ACT.Ln, bias=1.0).then_inc(log_done, 1)

                def h(n):
                    b, c = BANKS[n], BANK_COLS[BANKS[n]]
                    act.wait_ge(sp_done, 3 * head + n + 1)
                    nc.scalar.activation(sp_hi[:, b, 0:c], sp[:, b, 0:c], ACT.Copy).then_inc(sphi_done, 1)

                for step, n in ((a, 0), (a, 1), (e, 0), (a, 2), (e, 1), (l, 0), (e, 2), (l, 1), (l, 2), (h, 0), (h, 1), (h, 2)):
                    step(n)

            def probabilities(head):
                act.wait_ge(cum_done, head + 1)
                for b in BANKS:
                    c = BANK_COLS[b]
                    nc.scalar.activation(prob[:, b, 0:c], z[:, b, 0:c], ACT.Exp).then_inc(prob_done, 1)

            def rows_out(buf, prompt, sample, i):
                n = bass.ds(i, 1)
                act.dma_start(prompt[0:4 * P, n, :].rearrange("(t p) n c -> p t (n c)", p=P), buf[:, 0:4, :]).then_inc(kv_out, 16)
                act.dma_start(prompt[4 * P:4 * P + META, n, :].rearrange("t n c -> t (n c)"), buf[0:META, 4, :]).then_inc(kv_out, 16)
                act.dma_start(sample[:, n, :].rearrange("t n c -> t (n c)"), buf[META:META + DEC, 4, :]).then_inc(kv_out, 16)

            def unturn(tile_n, dst):
                act.wait_ge(tile_done, tile_n)
                nc.scalar.activation(dst[:, 0:4, :].rearrange("p t c -> p (t c)"), dense[:, 1, 0, :], ACT.Copy)
                return nc.scalar.activation(dst[:, 4, :], dense[:, 1, 1, 0:P], ACT.Copy)

            def attn_gate(i):
                log_sigmoid_parts(psum2(1, HALFO), gate_a[:], HALFO, tile(i, T_G) + 1, ga_abs, ga_exp, ga_ln, i + 1)

            def attn_gate_end(i):
                act.wait_ge(ga_log, i + 1)
                nc.scalar.activation(gate_a[:], gate_a[:], ACT.Exp).then_inc(ga_done, 1)

            def keys_out(i, wait):
                if wait:
                    act.wait_ge(kv_out, 16 * (8 * i + 3))
                unturn(tile(i, T_KT) + 1, k_tok)
                nc.scalar.activation(glu_tok[:], dense[0:92, 1, 1, P:2 * P], ACT.Copy).then_inc(ktok_kept, 1)
                act.wait_ge(ktok_kept, i + 1)
                rows_out(k_tok, nkp, nks, i)
                act.dma_start(ncp[:, bass.ds(i, 1), :].rearrange("t n c -> t (n c)"), glu_tok[0:PAD, :]).then_inc(kv_out, 16)
                act.dma_start(ncs[:, bass.ds(i, 1), :].rearrange("t n c -> t (n c)"), glu_tok[92 - PAD:92, :]).then_inc(kv_out, 16)

            def turn(i, prev=None):
                first = prev is None
                def high_ahead(u):
                    before = u - RING_LOOP
                    if before < 0:
                        free = None if first else tile(prev, UNIT_TILE[before + LOOP_UNITS]) + 1
                    else:
                        free = KC + 1 if first and before == 0 else tile(i, UNIT_TILE[before]) + 1
                    high(u % RING_LOOP, raw_loop[u % LOOP_UNITS], 16 * (i + 1 + u // LOOP_UNITS), free)

                high_ahead(2)
                if not first:
                    attn_gate(prev)
                act.wait_ge(tile_done, KC + 1 if first else tile(prev, T_Q_NEXT) + 1)
                nc.scalar.activation(cols2(qT[:], HALFO), psum2(0, HALFO), ACT.Copy, scale=HD ** -0.5).then_inc(q_kept, 1)
                high_ahead(3)
                if not first:
                    attn_gate_end(prev)
                    keys_out(prev, True)
                    probabilities(2 * i - 1)
                high_ahead(4)
                act.wait_ge(tile_done, tile(i, T_CT) + 1)
                nc.scalar.activation(ckT[:], dense[:, 0, 0, 0:2 * P], ACT.Copy).then_inc(ckT_kept, 1)
                softplus_logs(2 * i)
                high_ahead(5)
                act.wait_ge(tile_done, tile(i, T_A) + 1)
                nc.scalar.activation(cols2(a_sb[:], HALF), psum2(0, HALF), ACT.Copy).then_inc(a_kept, 1)
                high_ahead(6)
                probabilities(2 * i)
                if not first:
                    act.wait_ge(kv_out, 16 * 8 * i)
                unturn(tile(i, T_VT) + 1, v_tok).then_inc(vtok_kept, 1)
                act.wait_ge(vtok_kept, i + 1)
                rows_out(v_tok, nvp, nvs, i)
                log_sigmoid_parts(psum2(0, HALF), gate_b[:], HALF, tile(i, T_B) + 1, gb_abs, gb_exp, gb_ln, i + 1)
                high_ahead(7)
                act.wait_ge(gb_log, i + 1)
                nc.scalar.activation(gate_b[:], gate_b[:], ACT.Exp).then_inc(gb_done, 1)
                softplus_logs(2 * i + 1)

            turn(0)
            with act.Fori(0, KC - 1) as before:
                turn(before + 1, before)

            def high_post(g, n):
                high((n + 2) % RING, raw_post[(n + 2) % RING], 16 * (g + 1), FIRST_POST + 4 * g + n - 1)

            def post_group(g, body, last=False):
                for n in range(4):
                    if not (last and n >= 2):
                        high_post(g, n)
                    body(n)

            def gate_conv(f, func):
                act.wait_ge(tile_done, FIRST_POST + f + 1)
                nc.scalar.activation(cols2(gate_c[:, f, :], HALFO), psum2(f % 2, HALFO), func).then_inc(emptied[f % 2], 1)

            def squares(ks):
                for k in ks:
                    act.wait_ge(centred, k + 1)
                    if k >= 2:
                        act.wait_ge(ssum_done, k - 1)
                    nc.scalar.activation(part[:, k % 2, :], yconv[:, k, :], ACT.Square).then_inc(ysq_done, 1)

            def silu(ks):
                for k in ks:
                    act.wait_ge(u_done, k + 1)
                    nc.scalar.activation(n32[:, k % 2, 0:OUTTOK], yconv[:, k, :], ACT.Silu, bias=vec(B_LN, k)).then_inc(silu_done, 1)
                    act.wait_ge(silu_done, k + 1)
                    nc.scalar.activation(s_hi[:, k, :], n32[:, k % 2, 0:OUTTOK], ACT.Copy).then_inc(nhi_done, 1)

            high_post(0, 0)
            attn_gate(KC - 1)
            attn_gate_end(KC - 1)
            keys_out(KC - 1, True)
            high_post(0, 1)
            probabilities(2 * KC - 1)
            act.preload_act_table_set("sigmoid_and_others")
            gate_conv(0, ACT.Sigmoid)
            high_post(0, 2)
            gate_conv(1, ACT.Sigmoid)
            high_post(0, 3)
            gate_conv(2, ACT.Sigmoid)
            high_post(1, 0)
            squares(range(0, 4))
            gate_conv(3, ACT.Sigmoid)
            high_post(1, 1)
            squares(range(4, KC))
            gate_conv(4, ACT.Sigmoid)
            high_post(1, 2)
            act.preload_act_table_set("natural_log_exp_and_others")
            gate_conv(5, ACT.Copy)
            high_post(1, 3)
            inverse_root(var_done, 1, 2, OUTTOK, HALFO)
            act.wait_ge(kv_out, 16 * 8 * KC)
            act.preload_act_table_set("silu_and_others")
            silu(range(0, 4))
            gate_conv(6, ACT.Copy)
            silu(range(4, KC))
            gate_conv(7, ACT.Copy)
            for f in (5, 6, 7):
                act.wait_ge(emptied[f % 2], KC // 2 + f // 2 + 1)
                nc.scalar.activation(gate_c[:, f, :], gate_c[:, f, :], ACT.Sigmoid).then_inc(gates_done, 1)

            def post(first, last, body):
                with act.Fori(first, last) as g:
                    post_group(g, lambda n: body(g, 4 * (g - first) + n, n))

            def merge(g, f, n):
                act.wait_ge(m_done, f + 1)
                nc.scalar.activation(r_hi[:, bass.ds(f, 1), 0:OUTTOK].rearrange("p n c -> p (n c)"), n32[:, n % 2, 0:OUTTOK], ACT.Copy).then_inc(mhi_done, 1)
            post(2, 4, merge)
            act.preload_act_table_set("natural_log_exp_and_others")

            def out_squares(g, f, n):
                fs = bass.ds(f, 1)
                x_cur = xT[:, fs, META:].rearrange("p n c -> p (n c)")
                act.wait_ge(emptied[n % 2], emptied_at(g, n))
                nc.scalar.activation(s_hi[:, fs, :].rearrange("p n c -> p (n c)"), x_cur, ACT.Copy, scale=vecs[:, bass.ds(G_MLP * KC + f, 1)]).then_inc(uhi_done, 1)
                nc.scalar.activation(n32[:, 0, 0:OUTTOK], x_cur, ACT.Square).then_inc(x2sq_done, 1)
                act.wait_ge(x2sum_done, f + 1)
            post(4, 6, out_squares)

            def up(g, f, n, half):
                U = 2 * KC * ((g0 - 6) // 8) + f
                act.wait_ge(emptied[n % 2], emptied_at(g, n))
                nc.scalar.activation(n32[:, n % 2, 0:OUTTOK], n32[:, n % 2, 0:OUTTOK], ACT.Square).then_inc(u32_done, 1)
                act.wait_ge(u32_done, U + 1)
                hi = (r_hi, u_hi)[half]
                nc.scalar.activation(hi[:, bass.ds(f - KC * half, 1), 0:OUTTOK].rearrange("p n c -> p (n c)"), n32[:, n % 2, 0:OUTTOK], ACT.Copy).then_inc(uhi_done, 1)

            for rr in range(2):
                g0 = 6 + 8 * rr
                if rr == 0:
                    high_post(6, 0)
                    inverse_root(ss2_done, 1, 3, OUTTOK, HALFO)
                    up(6, 0, 0, 0)
                    for n in range(1, 4):
                        high_post(6, n)
                        up(6, n, n, 0)
                with act.Fori(7 if rr == 0 else 14, g0 + 2) as g:
                    post_group(g, lambda n: up(g, 4 * (g - g0) + n, n, 0))
                with act.Fori(g0 + 2, g0 + 4) as g:
                    post_group(g, lambda n: up(g, 4 * (g - g0) + n, n, 1))
                if rr == 0:
                    with act.Fori(10, 14) as g:
                        post_group(g, lambda n: None)
            with act.Fori(18, 20) as g:
                post_group(g, lambda n: None)

            def half_back(t):
                act.wait_ge(turned, 4)
                nc.scalar.activation(y_tok[:, t, 0:D // 2], pv[:] if t == 3 else z[:, t], ACT.Copy).then_inc(half_kept, 1)

            for f in range(KC):
                g, n = 20 + f // 4, f % 4
                if f < KC - 2:
                    high_post(g, n)
                act.wait_ge(emptied[n % 2], emptied_at(g, n))
                if f >= 1:
                    act.wait_ge(x2sum_done, KC + f)
                nc.scalar.activation(n32[:, 0, 0:OUTTOK], xT[:, f, META:], ACT.Square).then_inc(x2sq_done, 1)
                act.wait_ge(x2sq_done, KC + f + 1)
                nc.scalar.activation(xT[:, f, META:], xT[:, f, META:], ACT.Copy, scale=vec(G_FINAL, f)).then_inc(xg_done, 1)
                if f == 4:
                    half_back(2)
                    half_back(3)
            act.wait_ge(ss2_done, 2)
            nc.scalar.activation(rstd_tok[:, 0:4], dense[:, 1, 0, 0:4], ACT.Ln, scale=1.0 / D, bias=eps_col[:, 0:1])
            nc.scalar.activation(rstd_tok[0:DEC, 4:5], dense[0:DEC, 1, 0, 4:5], ACT.Ln, scale=1.0 / D, bias=eps_col[0:DEC, 0:1]).then_inc(ln_step, 1)
            act.wait_ge(ln_step, 4)
            nc.scalar.activation(rstd_tok[:, 0:4], rstd_tok[:, 0:4], ACT.Exp, scale=-0.5)
            nc.scalar.activation(rstd_tok[0:DEC, 4:5], rstd_tok[0:DEC, 4:5], ACT.Exp, scale=-0.5).then_inc(rstd_done, 1)
            act.wait_ge(rstd_done, 4)
            for t in (2, 3):
                nc.scalar.activation(y_tok[:, t, D // 2:], pv[:] if t == 3 else z[:, t], ACT.Copy, scale=rstd_tok[:, t:t + 1]).then_inc(y_by_act, 1)
                nc.scalar.activation(y_tok[:, t, 0:D // 2], y_tok[:, t, 0:D // 2], ACT.Copy, scale=rstd_tok[:, t:t + 1]).then_inc(y_by_act, 1)
            nc.scalar.activation(y_tok[0:DEC, 4, D // 2:], dense[0:DEC, 0, 1, :], ACT.Copy, scale=rstd_tok[0:DEC, 4:5]).then_inc(y_by_act, 1)

        @block.vector
        def _(dve):
            nc.vector.memset(eps_col[:], EPS).then_inc(eps_set, 1)
            dve.wait_ge(rows_turned, 1)
            nc.vector.tensor_copy(vecs[:], z[:, 1, 0:6 * KC]).then_inc(rows_kept, 1)
            for k in range(KC):
                dve.wait_ge(tile_done, k + 1)
                nc.vector.tensor_copy(xT[:, k, 0:512], dense[:, k % 2, 0, :])
                nc.vector.tensor_copy(xT[:, k, 512:TOK], dense[:, k % 2, 1, 0:TOK - 512]).then_inc(emptied[k % 2], 1)

            def normalise():
                for k in range(KC + 1):
                    if k < KC:
                        if k >= 2:
                            dve.wait_ge(r_ready, k - 1)
                        nc.vector.scalar_tensor_tensor(n32[:, k % 2, :], xT[:, k, :], vec(G_MIX, k), rstd[:], ALU.mult, ALU.mult).then_inc(n32_done, 1)
                    if k >= 1:
                        dve.wait_ge(nhi_done, k)
                        nc.vector.tensor_tensor(r_lo[:, k - 1, :], n32[:, (k - 1) % 2, :], r_hi[:, k - 1, :].bitcast(F32), ALU.subtract).then_inc(r_ready, 1)

            dve.wait_ge(rows_kept, 2)
            dve.wait_ge(emptied[1], KC // 2)
            dve.wait_ge(rstd_done, 1)
            normalise()
            dve.wait_ge(zeroed, 4)

            def conv(i, taps):
                for k in taps:
                    src, w, dst = conv_in[:, META + k:META + k + CONV_COLS], cw_cur[:, PAD + k:PAD + k + 1], acc[:, k % 2, :]
                    if k < 2:
                        nc.vector.tensor_scalar(dst, src, w, None, ALU.mult).then_inc(tap_done, 1)
                    else:
                        dve.wait_ge(tap_done, TAPS * i + k - 1)
                        nc.vector.scalar_tensor_tensor(dst, src, w, dst, ALU.mult, ALU.add).then_inc(tap_done, 1)

            def gate_mix(i):
                mixed_cur = mixed[:, bass.ds(i, 1), :].rearrange("p n c -> p (n c)")
                dve.wait_ge(ga_done, i + 1)
                dve.wait_ge(pv_done, 2 * (i + 1))
                nc.vector.tensor_tensor(mixed_cur[:, SEQ:], z[:, 1, S_PV:S_PV + DEC], gate_a[:, SEQ:], ALU.mult).then_inc(mix_s_done, 1)
                nc.vector.tensor_tensor(mixed_cur[:, 0:SEQ], pv[:], gate_a[:, 0:SEQ], ALU.mult).then_inc(mix_done, 1)

            def attn_gate(i):
                dve.wait_ge(ga_ln, i + 1)
                nc.vector.scalar_tensor_tensor(cols2(gate_a[:], HALFO), psum2(1, HALFO), 0.0, cols2(gate_a[:], HALFO), ALU.min, ALU.subtract).then_inc(ga_log, 1)

            def conv_end(i):
                y_cur = yconv[:, bass.ds(i, 1), :].rearrange("p n c -> p (n c)")
                dve.wait_ge(tap_done, TAPS * (i + 1))
                nc.vector.scalar_tensor_tensor(y_cur[:, 0:SEQ], acc[:, 0, 0:SEQ], bdw_cur[:, 0:1], acc[:, 1, 0:SEQ], ALU.add, ALU.add)
                nc.vector.scalar_tensor_tensor(y_cur[:, SEQ:], acc[:, 0, CONV_COLS - DEC:], bdw_cur[:, 0:1], acc[:, 1, CONV_COLS - DEC:], ALU.add, ALU.add).then_inc(y_done, 1)
                dve.wait_ge(y_done, i + 1)
                nc.vector.tensor_tensor(sum_y[:], sum_y[:], y_cur, ALU.add).then_inc(sumy_done, 1)

            CONV = [range(0, 2), range(2, 4), range(4, 7), range(7, 22), range(22, 24), range(24, 25), range(25, 26), range(26, TAPS)]

            def turn(i, prev=None):
                first = prev is None
                def conv_before(n):
                    if not first:
                        conv(prev, CONV[n])

                def softplus_sum(head, n):
                    b, c = BANKS[n], BANK_COLS[BANKS[n]]
                    dve.wait_ge(log_done, 3 * head + n + 1)
                    nc.vector.scalar_tensor_tensor(sp[:, b, 0:c], z[:, b, 0:c], 0.0, ez[:, b, 0:c], ALU.max, ALU.add).then_inc(sp_done, 1)

                def softplus_low(head, n):
                    b, c = BANKS[n], BANK_COLS[BANKS[n]]
                    dve.wait_ge(sphi_done, 3 * head + n + 1)
                    nc.vector.tensor_tensor(sp_lo[:, b, 0:c], sp[:, b, 0:c], sp_hi[:, b, 0:c].bitcast(F32), ALU.subtract).then_inc(splo_done, 1)

                def keep_keys(t, slot, dst, kept):
                    dve.wait_ge(tile_done, tile(i, t) + 1)
                    nc.vector.tensor_copy(cols2(dst[:, 0:TOK], HALF), psum2(slot, HALF))
                    nc.vector.tensor_copy(dst[:, TOK:TOK + META], dense[:, slot, 0, 0:META]).then_inc(kept, 1)

                conv_before(2)
                if not first:
                    attn_gate(prev)
                conv_before(3)
                keep_keys(T_K, 1, kT, k_kept)
                conv_before(4)
                if not first:
                    gate_mix(prev)
                for n in range(3):
                    softplus_sum(2 * i, n)
                    if n < 2:
                        conv_before(5 + n)
                for n in range(3):
                    softplus_low(2 * i, n)
                keep_keys(T_V, 1, vT, v_kept)
                conv_before(7)
                if not first:
                    conv_end(prev)
                n = bass.ds(i, 1)
                nc.vector.tensor_copy(cw_cur[:], cw[:, n, :].rearrange("p n c -> p (n c)"))
                nc.vector.tensor_copy(bdw_cur[:], vecs[:, bass.ds(B_DW * KC + i, 1)])
                nc.vector.tensor_copy(conv_in[:, CTX_CACHE:CTX_S], cw[:, n, 0:PAD].rearrange("p n c -> p (n c)")).then_inc(cur_done, 1)
                dve.wait_ge(gb_ln, i + 1)
                nc.vector.scalar_tensor_tensor(cols2(gate_b[:], HALF), psum2(0, HALF), 0.0, cols2(gate_b[:], HALF), ALU.min, ALU.subtract).then_inc(gb_log, 1)
                dve.wait_ge(gb_done, i + 1)
                nc.vector.tensor_tensor(conv_in[:, PAD:CTX_CACHE], a_sb[:, 0:META + SEQ], gate_b[:, 0:META + SEQ], ALU.mult)
                nc.vector.tensor_tensor(conv_in[:, CTX_S:], a_sb[:, META + SEQ:], gate_b[:, META + SEQ:], ALU.mult).then_inc(glu_done, 1)
                dve.wait_ge(glu_done, i + 1)
                dve.wait_ge(cur_done, i + 1)
                for n in range(3):
                    if n < 2:
                        conv(i, CONV[n])
                    softplus_sum(2 * i + 1, n)
                for n in range(3):
                    softplus_low(2 * i + 1, n)

            turn(0)
            with dve.Fori(0, KC - 1) as before:
                turn(before + 1, before)
            attn_gate(KC - 1)
            for taps in CONV[2:]:
                conv(KC - 1, taps)
            gate_mix(KC - 1)
            conv_end(KC - 1)

            dve.wait_ge(mean_done, 1)
            nc.vector.tensor_scalar(cols2(rstd[:, 0:OUTTOK], HALFO), z[:, 0:2, 0:HALFO], 1.0 / D, None, ALU.mult).then_inc(mean_kept, 1)
            dve.wait_ge(mean_kept, 1)
            nc.vector.memset(sum_sq[:], 0.0).then_inc(mean_kept, 1)
            dve.wait_ge(mean_kept, 2)
            for k in range(KC + 1):
                if k < KC:
                    nc.vector.tensor_tensor(yconv[:, k, :], yconv[:, k, :], rstd[:, 0:OUTTOK], ALU.subtract).then_inc(centred, 1)
                if k >= 1:
                    dve.wait_ge(ysq_done, k)
                    if k >= 2:
                        dve.wait_ge(ssum_done, k - 1)
                    nc.vector.tensor_tensor(sum_sq[:], sum_sq[:], part[:, (k - 1) % 2, :], ALU.add).then_inc(ssum_done, 1)
            dve.wait_ge(rstd_done, 2)
            for k in range(KC + 1):
                if k < KC:
                    nc.vector.scalar_tensor_tensor(yconv[:, k, :], yconv[:, k, :], vec(G_LN, k), rstd[:, 0:OUTTOK], ALU.mult, ALU.mult).then_inc(u_done, 1)
                if k >= 1:
                    dve.wait_ge(nhi_done, KC + k)
                    nc.vector.tensor_tensor(s_lo[:, k - 1, :], n32[:, (k - 1) % 2, 0:OUTTOK], s_hi[:, k - 1, :].bitcast(F32), ALU.subtract).then_inc(s_ready, 1)

            with dve.Fori(2, 4) as g:
                for n in range(4):
                    f = 4 * (g - 2) + n
                    fs = bass.ds(f, 1)
                    flat = "p n c -> p (n c)"
                    dve.wait_ge(tile_done, FIRST_POST + 4 * g + n + 1)
                    if n == 0:
                        dve.wait_ge(gates_done, 3)
                    nc.vector.tensor_tensor(cols2(part[:, n % 2, :], HALFO), psum2(n % 2, HALFO), cols2(gate_c[:, fs, :].rearrange(flat), HALFO), ALU.mult)\
                        .then_inc(emptied[n % 2], 1)
                    dve.wait_ge(emptied[n % 2], emptied_at(g, n))
                    nc.vector.tensor_tensor(n32[:, n % 2, 0:OUTTOK], part[:, n % 2, :], mixed[:, fs, :].rearrange(flat), ALU.add).then_inc(m_done, 1)
                    dve.wait_ge(mhi_done, f + 1)
                    nc.vector.tensor_tensor(r_lo[:, fs, 0:OUTTOK].rearrange(flat), n32[:, n % 2, 0:OUTTOK], r_hi[:, fs, 0:OUTTOK].rearrange(flat).bitcast(F32), ALU.subtract)\
                        .then_inc(m_ready, 1)

            def residual(tile_n, slot, x_cur):
                dve.wait_ge(tile_done, tile_n)
                nc.vector.tensor_tensor(cols2(x_cur, HALFO), psum2(slot, HALFO), cols2(x_cur, HALFO), ALU.add).then_inc(emptied[slot], 1)

            def add_square(count):
                dve.wait_ge(x2sq_done, count)
                nc.vector.tensor_tensor(n32[:, 1, 0:OUTTOK], n32[:, 1, 0:OUTTOK], n32[:, 0, 0:OUTTOK], ALU.add).then_inc(x2sum_done, 1)

            dve.wait_ge(m_ready, KC)
            nc.vector.memset(n32[:, 1, :], 0.0).then_inc(mean_kept, 1)
            dve.wait_ge(mean_kept, 3)
            with dve.Fori(4, 6) as g:
                for n in range(4):
                    f = 4 * (g - 4) + n
                    fs = bass.ds(f, 1)
                    x_cur = xT[:, fs, META:].rearrange("p n c -> p (n c)")
                    residual(FIRST_POST + 4 * g + n + 1, n % 2, x_cur)
                    dve.wait_ge(uhi_done, f + 1)
                    nc.vector.scalar_tensor_tensor(s_lo[:, fs, :].rearrange("p n c -> p (n c)"), x_cur, vecs[:, bass.ds(G_MLP * KC + f, 1)],
                                                   s_hi[:, fs, :].rearrange("p n c -> p (n c)").bitcast(F32), ALU.mult, ALU.subtract).then_inc(h2_ready, 1)
                    add_square(f + 1)

            def up(g, g0, n, half):
                f = 4 * (g - g0) + n
                U = 2 * KC * ((g0 - 6) // 8) + f
                tile_n = FIRST_POST + 4 * g + n + 1
                dve.wait_ge(tile_done, tile_n)
                nc.vector.scalar_tensor_tensor(cols2(n32[:, n % 2, 0:OUTTOK], HALFO), psum2(n % 2, HALFO), 0.0, cols2(rstd[:, 0:OUTTOK], HALFO), ALU.max, ALU.mult)\
                    .then_inc(emptied[n % 2], 1)
                dve.wait_ge(uhi_done, KC + U + 1)
                fs = bass.ds(f - KC * half, 1)
                hi, lo = ((r_hi, r_lo), (u_hi, u_lo))[half]
                nc.vector.tensor_tensor(lo[:, fs, 0:OUTTOK].rearrange("p n c -> p (n c)"), n32[:, n % 2, 0:OUTTOK],
                                        hi[:, fs, 0:OUTTOK].rearrange("p n c -> p (n c)").bitcast(F32), ALU.subtract).then_inc(u_ready, 1)

            dve.wait_ge(rstd_done, 3)
            for rr in range(2):
                g0 = 6 + 8 * rr
                for half in range(2):
                    with dve.Fori(g0 + 2 * half, g0 + 2 * half + 2) as g:
                        for n in range(4):
                            up(g, g0, n, half)
                for half in range(2 if rr == 0 else 1):
                    with dve.Fori(g0 + 4 + 2 * half, g0 + 6 + 2 * half) as g:
                        for n in range(4):
                            f = 4 * (g - g0 - 4 - 2 * half) + n
                            residual(FIRST_POST + 4 * g + n + 1, n % 2, xT[:, bass.ds(f, 1), META:].rearrange("p n c -> p (n c)"))
            dve.wait_ge(u_ready, 4 * KC)
            nc.vector.memset(n32[:, 1, :], 0.0).then_inc(mean_kept, 1)
            dve.wait_ge(mean_kept, 4)
            for f in range(KC):
                residual(FIRST_POST + 4 * 20 + f + 1, f % 2, xT[:, f, META:])
                add_square(KC + f + 1)
                if f == 4:
                    dve.wait_ge(turned, 4)
                    for t in (0, 1):
                        nc.vector.tensor_copy(y_tok[:, t, 0:D // 2], z[:, t]).then_inc(half_kept, 1)
            dve.wait_ge(rstd_done, 4)
            dve.wait_ge(half_kept, 4)
            dve.wait_ge(turned, KC + 1)
            for t in (0, 1):
                nc.vector.tensor_scalar(y_tok[:, t, D // 2:], z[:, t], rstd_tok[:, t:t + 1], None, ALU.mult).then_inc(y_by_dve, 1)
                nc.vector.tensor_scalar(y_tok[:, t, 0:D // 2], y_tok[:, t, 0:D // 2], rstd_tok[:, t:t + 1], None, ALU.mult).then_inc(y_by_dve, 1)
            nc.vector.tensor_scalar(y_tok[0:DEC, 4, 0:D // 2], dense[0:DEC, 0, 0, :], rstd_tok[0:DEC, 4:5], None, ALU.mult).then_inc(y_by_dve, 1)


_INS = ["x_prompt", "x_sample", "cache_k", "cache_v", "cache_conv", "meta", "g_mix", "w_in", "w_dw", "b_dw",
        "g_ln_conv", "b_ln_conv", "w_pw2", "w_out", "g_mlp", "w_up", "w_down", "g_final"]
_OUTS = [(1, SEQ, D), (1, DEC, D), (1, 1, META + SEQ, HEADS, HD), (1, 1, META + SEQ, HEADS, HD), (1, 1, PAD, D),
         (1, 1, DEC, HEADS, HD), (1, 1, DEC, HEADS, HD), (1, 1, PAD, D)]


def kernel(**inputs):
    import numpy as _np
    import concourse.bacc as _bacc
    from concourse.bass_utils import run_bass_kernel_spmd as _run

    nc = _bacc.Bacc("TRN2", target_bir_lowering=False, num_devices=1)
    arrays, args = {}, []
    for name in _INS:
        a = _np.ascontiguousarray(inputs[name])
        arrays[f"in_{name}_dram"] = a
        args.append(nc.dram_tensor(f"in_{name}_dram", a.shape, mybir.dt.from_np(a.dtype), kind="ExternalInput").ap())
    for n, shape in enumerate(_OUTS):
        args.append(nc.dram_tensor(f"out_{n}_dram", shape, F32, kind="ExternalOutput").ap())
    build(nc, *args)
    r = _run(nc, [arrays], core_ids=[0])
    return tuple(r.results[0][f"out_{n}_dram"] for n in range(len(_OUTS)))
```

```python
from contextlib import ExitStack

import concourse.bass as bass
from concourse import mybir

P = 128
ACT = mybir.ActivationFunctionType
ALU = mybir.AluOpType
F32 = mybir.dt.float32
F32R = mybir.dt.float32r
BF16 = mybir.dt.bfloat16

D = 1024
KC = D // P
HEADS, HD = 16, 64
META, SEQ, DEC = 16, 512, 32
TAPS = 31
PAD = TAPS - 1
EPS = 1e-6
TOK = META + SEQ + DEC
OUTTOK = SEQ + DEC
HALF, HALFO = TOK // 2, OUTTOK // 2
KEYS = 5 * P
NEG = -1e30

LOOP_UNITS = 6
N_LOOP = KC * LOOP_UNITS
RING_LOOP, RING = 3, 4
GROUPS_PER_STAGE = KC // 4
ROUNDS = 4
N_GROUPS = (3 + 2 * ROUNDS) * GROUPS_PER_STAGE

T_Q, T_K, T_KC, T_V, T_VT, T_A, T_B, T_G = range(8)
LOOP_TILES = 8
X_TILES = 5
X_EMPTIED = (3, 2)
FIRST_POST = X_TILES + KC * LOOP_TILES + 1

WARM_UP = 16

KT = [(0, 0, 512, 0), (1, 0, 400, 112), (2, 0, 272, 240), (2, 304, 144, 368)]
LAST, N_LAST = (1, 400), META + DEC
S_CACHE0, S_CACHE1, S_OWN = (2, 272), (2, 448), (1, 416)
BANKS = (0, 2, 1)
BANK_COLS = (512, 448, 480)
S_PV = 448


def build(nc, x_prompt, x_sample, cache_k, cache_v, cache_conv, meta, g_mix, w_in, w_dw, b_dw,
          g_ln_conv, b_ln_conv, w_pw2, w_out, g_mlp, w_up, w_down, g_final,
          y_prompt, y_sample, new_k_prompt, new_v_prompt, new_conv_prompt,
          new_k_sample, new_v_sample, new_conv_sample):
    xp, xs = x_prompt[0], x_sample[0]

    def weight(w, name):
        return w.rearrange("(k p) (n c) -> p k n c", p=P, c=P)

    win_v = weight(w_in[0], "in")
    wpw_v = weight(w_pw2[0], "pw2")
    wout_v = weight(w_out[0], "out")
    wup_v = weight(w_up[0], "up")
    wdown_v = w_down[0].rearrange("(r k p) (n c) -> p r k n c", p=P, k=KC, c=P)
    ck_v = cache_k[0, 0].rearrange("(t p) h d -> p t (h d)", p=P).rearrange("p t (n c) -> p t n c", c=P)
    cv_v = cache_v[0, 0].rearrange("(t p) h d -> p t (h d)", p=P).rearrange("p t (n c) -> p t n c", c=P)

    def rows(o):
        return o[0, 0].rearrange("t h d -> t (h d)").rearrange("t (n c) -> t n c", c=P)

    nkp, nvp, nks, nvs = rows(new_k_prompt), rows(new_v_prompt), rows(new_k_sample), rows(new_v_sample)
    ncp = new_conv_prompt[0, 0].rearrange("t (n c) -> t n c", c=P)
    ncs = new_conv_sample[0, 0].rearrange("t (n c) -> t n c", c=P)

    with ExitStack() as ctx:
        def sb(name, shape, dt=F32, where=ctx):
            return where.enter_context(nc.sbuf_tensor(name, shape, dt))

        def sem(name):
            return ctx.enter_context(nc.semaphore(name))

        w_raw = sb("w_raw", [P, RING, KC, P])
        w_hi = sb("w_hi", [P, RING, KC, P], F32R)
        w_lo = sb("w_lo", [P, RING, KC, P], F32R)
        xT = sb("xT", [P, KC, TOK])
        r_hi = sb("r_hi", [P, KC, TOK], F32R)
        r_lo = sb("r_lo", [P, KC, TOK], F32R)
        ident = sb("ident", [P, P])
        ident_b = sb("ident_b", [P, P], BF16)
        ones = sb("ones", [P, P])
        tri = sb("tri", [P, P], F32R)
        negones = sb("negones", [P, P], F32R)
        own_all = sb("own_all", [P, P], F32R)
        own_own = sb("own_own", [P, P], F32R)
        cache_meta = sb("cache_meta", [P, P], F32R)
        neg_diag = sb("neg_diag", [P, P], BF16)
        neg_last = sb("neg_last", [P, N_LAST], BF16)
        cw = sb("cw", [P, KC, PAD + TAPS])
        vecs = sb("vecs", [P, 6 * KC])
        eps_col = sb("eps_col", [P, 1])
        rstd_tok = sb("rstd_tok", [P, 5])
        rstd = sb("rstd", [P, TOK])
        keys = ExitStack()
        k_hi = sb("k_hi", [P, TOK], F32R, where=keys)
        k_lo = sb("k_lo", [P, TOK], F32R, where=keys)
        keys.close()
        n32 = sb("n32", [P, 2, TOK])

        sq = n32[:].rearrange("p a c -> p (a c)")[:, 0:D]
        S1, S2, CC = slice(0, 400), slice(400, 672), slice(672, 704)
        SUMS = 704

        def ring_end(buf):
            return buf[:, RING_LOOP].rearrange("p k c -> p (k c)")[:, 0:SUMS]
        sums, sums_hi, sums_lo = ring_end(w_raw), ring_end(w_hi), ring_end(w_lo)

        def vec(n, k):
            return vecs[:, n * KC + k:n * KC + k + 1]
        G_MIX, B_DW, G_LN, B_LN, G_MLP, G_FINAL = range(6)

        late = ExitStack()
        u_hi = sb("u_hi", [P, KC, OUTTOK], F32R, where=late)
        u_lo = sb("u_lo", [P, KC, OUTTOK], F32R, where=late)
        late.close()
        mid = ExitStack()
        yconv = sb("yconv", [P, KC, OUTTOK], where=mid)
        mixed = sb("mixed", [P, KC, OUTTOK], where=mid)
        sum_y = sb("sum_y", [P, OUTTOK], where=mid)

        loop = ExitStack()
        vT = sb("vT", [P, KEYS], where=loop)
        ck_tok = sb("ck_tok", [P, 2, P], where=loop)
        start = ExitStack()
        x_tok = sb("x_tok", [P, 5, D], where=start)
        cw_rows = sb("cw_rows", [PAD + TAPS, D], where=start)
        vec_rows = sb("vec_rows", [6 * KC, P], where=start)
        mat_f = sb("mat_f", [P, 5, P], where=start)
        diag = sb("diag", [P, 5, P], where=start)
        start.close()
        qT = sb("qT", [P, OUTTOK], where=loop)
        ckT = sb("ckT", [P, 2 * P], where=loop)
        a_sb = sb("a_sb", [P, TOK], where=loop)
        gate_b = sb("gate_b", [P, TOK], where=loop)
        sp = sb("sp", [P, 3, 512], where=loop)
        ez = sb("ez", [P, 3, 512], where=loop)
        sp_hi = sb("sp_hi", [P, 3, 512], F32R, where=loop)
        sp_lo = sb("sp_lo", [P, 3, 512], F32R, where=loop)
        prob = ez
        kT = sb("kT", [P, KEYS], where=loop)
        v_tok = sb("v_tok", [P, 5, P], where=loop)
        k_tok = sb("k_tok", [P, 5, P], where=loop)
        glu_tok = sb("glu_tok", [92, P], where=loop)
        cv_tok = sb("cv_tok", [P, 2, P], where=loop)
        CTX_CACHE = PAD + META + SEQ
        CTX_S = CTX_CACHE + PAD
        CONV_COLS = CTX_S + DEC - META - PAD
        conv_in = sb("conv_in", [P, CTX_S + DEC], where=loop)
        acc = sb("acc", [P, 2, CONV_COLS], where=loop)
        cw_cur = sb("cw_cur", [P, PAD + TAPS], where=loop)
        bdw_cur = sb("bdw_cur", [P, 1], where=loop)
        gate_a = sb("gate_a", [P, OUTTOK], where=loop)
        q_hi = sb("q_hi", [P, OUTTOK], F32R, where=loop)
        q_lo = sb("q_lo", [P, OUTTOK], F32R, where=loop)
        loop.close()

        post = ExitStack()
        gate_c = sb("gate_c", [P, KC, OUTTOK], where=post)
        part = sb("part", [P, 2, OUTTOK], where=post)
        sum_sq = sb("sum_sq", [P, OUTTOK], where=post)
        rows_back = ExitStack()
        y_tok = sb("y_tok", [P, 5, D], where=rows_back)
        rows_back.close()
        s_hi = sb("s_hi", [P, KC, OUTTOK], F32R, where=post)
        s_lo = sb("s_lo", [P, KC, OUTTOK], F32R, where=post)
        post.close()
        mid.close()

        dense = ctx.enter_context(nc.psum_tensor("dense", [P, 2, 2, 512], F32))
        z = ctx.enter_context(nc.psum_tensor("z", [P, 3, 512], F32))
        pv = ctx.enter_context(nc.psum_tensor("pv", [P, 512], F32))

        x_loaded = [sem(f"x_loaded{t}") for t in range(X_TILES)]
        rows_loaded = sem("rows_loaded")
        raw_loop = [sem(f"raw_loop{n}") for n in range(LOOP_UNITS)]
        raw_post = [sem(f"raw_post{n}") for n in range(4)]
        ck_loaded, cv_loaded = sem("ck_loaded"), sem("cv_loaded")
        hi_done, lo_done = sem("hi_done"), sem("lo_done")
        tile_done = sem("tile_done")
        emptied = [sem("emptied0"), sem("emptied1")]
        consts, mats = sem("consts"), sem("mats")
        rows_turned, rows_kept = sem("rows_turned"), sem("rows_kept")
        sq_done, root_done, diag_done, spread = (sem(n) for n in ("sq_done", "root_done", "diag_done", "spread"))
        sums_step, sums_done, sumshi_done = sem("sums_step"), sem("sums_done"), sem("sumshi_done")
        eps_set, mean_kept = sem("eps_set"), sem("mean_kept")
        ln_step, rstd_done = sem("ln_step"), sem("rstd_done")
        n32_done, nhi_done, r_ready = sem("n32_done"), sem("nhi_done"), sem("r_ready")
        cur_done = sem("cur_done")
        r_ready_pool, qhi_done, khi_done = sem("r_ready_pool"), sem("qhi_done"), sem("khi_done")
        a_kept, gb_abs, gb_exp, gb_ln, gb_log, gb_done = (sem(n) for n in ("a_kept", "gb_abs", "gb_exp", "gb_ln", "gb_log", "gb_done"))
        ga_abs, ga_exp, ga_ln, ga_log, ga_done = (sem(n) for n in ("ga_abs", "ga_exp", "ga_ln", "ga_log", "ga_done"))
        glu_done, tap_done, y_done = sem("glu_done"), sem("tap_done"), sem("y_done")
        q_kept, ckT_kept, k_kept, v_kept = sem("q_kept"), sem("ckT_kept"), sem("k_kept"), sem("v_kept")
        vtok_kept, ktok_kept = sem("vtok_kept"), sem("ktok_kept")
        z_scored, abs_done, exp_done, log_done = sem("z_scored"), sem("abs_done"), sem("exp_done"), sem("log_done")
        sp_done, sphi_done, splo_done = sem("sp_done"), sem("sphi_done"), sem("splo_done")
        cum_done, prob_done, pv_done = sem("cum_done"), sem("prob_done"), sem("pv_done")
        mix_s_done, mix_done, gates_done = sem("mix_s_done"), sem("mix_done"), sem("gates_done")
        kv_out = sem("kv_out")
        sumy_done, mean_done, centred, ysq_done, ssum_done = (sem(n) for n in ("sumy_done", "mean_done", "centred", "ysq_done", "ssum_done"))
        var_done, u_done, silu_done, s_ready = (sem(n) for n in ("var_done", "u_done", "silu_done", "s_ready"))
        m_done, mhi_done, m_ready = (sem(n) for n in ("m_done", "mhi_done", "m_ready"))
        x2sq_done, x2sum_done, ss2_done = (sem(n) for n in ("x2sq_done", "x2sum_done", "ss2_done"))
        h2_ready, u32_done, uhi_done, u_ready = (sem(n) for n in ("h2_ready", "u32_done", "uhi_done", "u_ready"))
        xg_done, turned, half_kept = sem("xg_done"), sem("turned"), sem("half_kept")
        y_by_dve, y_by_act, y_out = sem("y_by_dve"), sem("y_by_act"), sem("y_out")
        zeroed = sem("zeroed")

        POOL_LOWS = (3, 6)

        def lows_before(k):
            by_pool = sum(c < k for c in POOL_LOWS)
            return k - by_pool, by_pool

        def tile(i, t):
            return X_TILES + LOOP_TILES * i + t

        UNIT_TILE = (T_Q, T_K, T_V, T_A, T_B, T_G)

        def emptied_at(g, n):
            return X_EMPTIED[n % 2] + 2 * g + n // 2 + 1

        def psum2(slot, half):
            return dense[:, slot, :, 0:half]

        def cols2(ap, half):
            return ap.rearrange("p (h c) -> p h c", c=half)

        block = ctx.enter_context(nc.Block())

        @block.sync
        def _(sync):
            for t, dst, src in ((0, x_tok[0:META, 0, :], meta), (0, x_tok[META:P, 0, :], xp[0:P - META]),
                                (1, x_tok[:, 1, :], xp[P - META:2 * P - META]), (2, x_tok[:, 2, :], xp[2 * P - META:3 * P - META]),
                                (3, x_tok[:, 3, :], xp[3 * P - META:4 * P - META]),
                                (4, x_tok[0:META, 4, :], xp[4 * P - META:SEQ]), (4, x_tok[META:META + DEC, 4, :], xs)):
                sync.dma_start(dst, src).then_inc(x_loaded[t], 16)
            for n, v in enumerate((g_mix, b_dw, g_ln_conv, b_ln_conv, g_mlp)):
                sync.dma_start(vec_rows[n * KC:(n + 1) * KC, :], v[0].rearrange("(k p) -> k p", p=P)).then_inc(rows_loaded, 16)
            sync.dma_start(vec_rows[5 * KC:, :], g_final.rearrange("(k p) -> k p", p=P)).then_inc(rows_loaded, 16)
            sync.dma_start(cw_rows[0:PAD, :], cache_conv[0, 0]).then_inc(rows_loaded, 16)
            sync.dma_start(cw_rows[PAD:, :], w_dw[0]).then_inc(rows_loaded, 16)

            BASE = [2 * KC, 3 * KC, 4 * KC, 0, KC, 6 * KC]

            def loads(i, first):
                for u in range(LOOP_UNITS):
                    if not (first and u < RING_LOOP):
                        sync.wait_ge(lo_done, LOOP_UNITS * i + u - 2)
                    sync.dma_start(w_raw[:, u % RING_LOOP], win_v[:, :, bass.ds(BASE[u] + i, 1), :].rearrange("p k n c -> p k (n c)")).then_inc(raw_loop[u], 16)
                    if u == 0:
                        if not first:
                            sync.wait_ge(ckT_kept, i)
                        sync.dma_start(ck_tok[:], ck_v[:, :, bass.ds(i, 1), :].rearrange("p t n c -> p t (n c)")).then_inc(ck_loaded, 16)
                    if u == 5:
                        if not first:
                            sync.wait_ge(pv_done, 2 * i)
                        sync.dma_start(cv_tok[:], cv_v[:, :, bass.ds(i, 1), :].rearrange("p t n c -> p t (n c)")).then_inc(cv_loaded, 16)

            loads(0, True)
            with sync.Fori(1, KC) as i:
                loads(i, False)

            for n in range(4):
                sync.wait_ge(lo_done, N_LOOP + n - 2)
                if n == RING_LOOP:
                    sync.wait_ge(splo_done, 4 * HEADS)
                sync.dma_start(w_raw[:, n], win_v[:, :, 5 * KC + n, :]).then_inc(raw_loop[n] if n < RING_LOOP else raw_post[n], 16)

            def load_group(g, view):
                for n in range(4):
                    sync.wait_ge(lo_done, N_LOOP + 4 * g + n - 3)
                    sync.dma_start(w_raw[:, n], view(n)).then_inc(raw_post[n], 16)

            load_group(1, lambda n: win_v[:, :, 5 * KC + 4 + n, :])
            for first_group, view in ((2, wpw_v), (4, wout_v)):
                with sync.Fori(0, 2) as j:
                    load_group(first_group + j, lambda n: view[:, :, bass.ds(4 * j + n, 1), :].rearrange("p k n c -> p k (n c)"))
            with sync.Fori(0, 2) as rr:
                with sync.Fori(0, 4) as j:
                    load_group(6 + 8 * rr + j, lambda n: wup_v[:, :, bass.ds(16 * rr + 4 * j + n, 1), :].rearrange("p k n c -> p k (n c)"))
                for half in range(2):
                    with sync.Fori(0, 2) as j:
                        load_group(10 + 2 * half + 8 * rr + j, lambda n: wdown_v[:, bass.ds(2 * rr + half, 1), :, bass.ds(4 * j + n, 1), :].rearrange("p r k n c -> p (r k) (n c)"))

            for t, done, count in ((0, y_by_dve, 2), (2, y_by_act, 2), (1, y_by_dve, 4), (3, y_by_act, 4)):
                sync.wait_ge(done, count)
                sync.dma_start(y_prompt[0, t * P:(t + 1) * P, :], y_tok[:, t, :]).then_inc(y_out, 16)
            sync.wait_ge(y_by_dve, 5)
            sync.wait_ge(y_by_act, 5)
            sync.dma_start(y_sample[0], y_tok[0:DEC, 4, :]).then_inc(y_out, 16)
            sync.wait_ge(y_out, 16 * 5)

        @block.gpsimd
        def _(pool):
            pool.memset(ident[:], 0.0).then_inc(consts, 1)
            pool.memset(ones[:], 1.0).then_inc(consts, 1)
            pool.memset(neg_diag[:], 0.0).then_inc(consts, 1)
            pool.memset(neg_last[:], 0.0).then_inc(consts, 1)
            pool.memset(mat_f[:], -1.0).then_inc(consts, 1)
            pool.memset(kT[:, TOK + META:KEYS], 0.0).then_inc(zeroed, 1)
            pool.memset(vT[:, TOK + META:KEYS], 0.0).then_inc(zeroed, 1)
            pool.memset(conv_in[:, 0:PAD], 0.0).then_inc(zeroed, 1)
            pool.memset(sum_y[:], 0.0).then_inc(zeroed, 1)
            done = 5

            def select(ap, pattern, base, mult, fill, op=ALU.is_ge):
                nonlocal done
                pool.wait_ge(consts, done)
                pool.affine_select(out=ap, in_=ap, pattern=pattern, compare_op=op, fill=fill, base=base, channel_multiplier=mult).then_inc(consts, 1)
                done += 1

            select(ident[:], [[-1, P]], 0, 1, 1.0, ALU.not_equal)
            select(neg_diag[:], [[1, P]], -1, -1, NEG)
            select(neg_last[:, 0:META], [[1, META]], -1, -1, NEG)
            neg_own = neg_last[:, META:]
            select(neg_own, [[1, DEC]], META - 1, -1, NEG)
            select(neg_own, [[0, DEC]], META + DEC - 1, -1, 0.0)
            select(neg_own, [[0, DEC]], META + DEC + META - 1, -1, NEG)
            select(neg_own, [[0, DEC]], -META, 1, NEG)
            M0 = META + DEC
            select(mat_f[:, 0, :], [[-1, P]], 0, 1, 0.0)
            select(mat_f[:, 2, :], [[0, P]], M0 - 1, -1, 0.0)
            select(mat_f[:, 3, 0:M0], [[-1, M0]], 0, 1, 0.0)
            select(mat_f[:, 3, 0:M0], [[0, M0]], M0 - 1, -1, 0.0)
            select(mat_f[:, 3, M0:P], [[0, P - M0]], M0 - 1, -1, 0.0)
            select(mat_f[:, 3, M0:P], [[1, P - M0]], M0 - 1, -1, -1.0)
            select(mat_f[:, 4, :], [[1, P]], -M0, 0, 0.0)
            pool.wait_ge(consts, done)
            pool.tensor_copy(ident_b[:], ident[:]).then_inc(mats, 1)
            for n, m in enumerate((tri, negones, own_all, own_own, cache_meta)):
                pool.tensor_copy(m[:], mat_f[:, n, :]).then_inc(mats, 1)

            def low(u, s):
                pool.wait_ge(hi_done, u + 1)
                pool.tensor_tensor(w_lo[:, s], w_raw[:, s], w_hi[:, s].bitcast(F32), ALU.subtract).then_inc(lo_done, 1)

            low(0, 0)
            low(1, 1)
            for k in POOL_LOWS:
                pool.wait_ge(nhi_done, k + 1)
                pool.tensor_tensor(r_lo[:, k, :], n32[:, k % 2, :], r_hi[:, k, :].bitcast(F32), ALU.subtract).then_inc(r_ready_pool, 1)
            low(2, 2)
            with pool.Fori(1, N_LOOP // RING_LOOP) as j:
                for s in range(RING_LOOP):
                    low(RING_LOOP * j + s, s)
            with pool.Fori(0, N_GROUPS) as g:
                for s in range(RING):
                    low(N_LOOP + RING * g + s, s)

        @block.tensor
        def _(pe):
            def claim(slot, n):
                pe.wait_ge(emptied[slot], n)

            def passes(wslot, slot, m_hi, m_lo, c0, half, k):
                for n, (w, m) in enumerate(((w_hi, m_hi), (w_hi, m_lo), (w_lo, m_hi))):
                    for h in range(2):
                        mm = nc.tensor.matmul(dense[:, slot, h, 0:half], w[:, wslot, k, :], m[:, k, c0 + h * half:c0 + (h + 1) * half],
                                              start=(k == 0 and n == 0), stop=(k == KC - 1 and n == 2))
                return mm

            def dense_unit(wslot, slot, m_hi, m_lo, c0, half, chunk_ready=None):
                for k in range(KC):
                    if chunk_ready is not None:
                        pe.wait_ge(chunk_ready[0], chunk_ready[1] + k)
                    mm = passes(wslot, slot, m_hi, m_lo, c0, half, k)
                mm.then_inc(tile_done, 1)

            pe.wait_ge(consts, 2)
            for _ in range(WARM_UP):
                nc.tensor.matmul(z[:, 0, 0:P], ones[:], ones[:], start=True, stop=True)
            pe.wait_ge(consts, 6)
            for t in range(X_TILES):
                n = P if t < 4 else META + DEC
                pe.wait_ge(x_loaded[t], 32 if t in (0, 4) else 16)
                if t >= 2:
                    claim(t % 2, t // 2)
                for k in range(KC):
                    mm = nc.tensor.transpose(dense[:, t % 2, k // 4, (k % 4) * P:(k % 4) * P + n], x_tok[0:n, t, k * P:(k + 1) * P], ident[0:n, 0:n])
                mm.then_inc(tile_done, 1)
            pe.wait_ge(rows_loaded, 16 * 8)
            for k in range(KC):
                nc.tensor.transpose(z[:, 0, k * 61:(k + 1) * 61], cw_rows[:, k * P:(k + 1) * P], ident[0:61, 0:61])
            nc.tensor.transpose(z[:, 1, 0:6 * KC], vec_rows[:], ident[0:6 * KC, 0:6 * KC]).then_inc(rows_turned, 1)
            for t in range(X_TILES):
                n = P if t < 4 else META + DEC
                pe.wait_ge(diag_done, t + 1)
                dst = z[:, 2, t * P:(t + 1) * P] if t < 4 else pv[:, 0:n]
                mm = nc.tensor.matmul(dst, ones[0:n, :], diag[0:n, t, 0:n], start=(t in (0, 4)), stop=True, skip_group_check=True)
            mm.then_inc(spread, 1)
            pe.wait_ge(rows_kept, 2)
            for _ in range(WARM_UP):
                nc.tensor.matmul(z[:, 0, 0:P], ones[:], ones[:], start=True, stop=True)
            pe.wait_ge(mats, 6)

            def scores(i, hh, first=False):
                r = slice(hh * HD, (hh + 1) * HD)
                if hh == 0:
                    pe.wait_ge(ckT_kept, i + 1)
                    pe.wait_ge(q_kept, i + 1)
                    pe.wait_ge(k_kept, i + 1)

                def score(bank, off, keys, q0, q1, start=False):
                    return nc.tensor.matmul(z[:, bank, off:off + q1 - q0], keys, qT[r, q0:q1], start=start, stop=False, skip_group_check=True)

                def score_split(bank, off, j, q0, start=False):
                    for n, (kp, qp) in enumerate(((k_hi, q_hi), (k_hi, q_lo), (k_lo, q_hi))):
                        nc.tensor.matmul(z[:, bank, off:off + SEQ - q0], kp[r, j * P:(j + 1) * P], qp[r, q0:SEQ], start=(start and n == 0), stop=False, skip_group_check=True)

                def mask(bank, off, m):
                    return nc.tensor.matmul(z[:, bank, off:off + m.shape[1]], ident_b[:], m, start=False, stop=False, skip_group_check=True)

                score(*S_CACHE0, ckT[r, 0:P], SEQ, OUTTOK, start=True)
                score(*S_CACHE1, ckT[r, P:2 * P], SEQ, OUTTOK)
                score_split(0, 0, 0, 0, start=True)
                mask(0, 0, neg_diag[:, META:P]).then_inc(z_scored, 1)
                for j in (2, 3):
                    bank, off, _, q0 = KT[j]
                    score_split(bank, off, j, q0)
                    mm = mask(bank, off, neg_diag[:])
                mm.then_inc(z_scored, 1)
                if hh == 0 and not first:
                    pe.wait_ge(mix_s_done, i)
                bank, off, _, q0 = KT[1]
                score_split(bank, off, 1, q0, start=True)
                mask(bank, off, neg_diag[:])
                score(*LAST, kT[r, 4 * P:5 * P], SEQ - META, OUTTOK)
                mask(*LAST, neg_last[:]).then_inc(z_scored, 1)

            def cumulate(head):
                pe.wait_ge(splo_done, 4 * head + 4)

                def add(m, dst, n, parts, src):
                    for part_ in parts:
                        mm = nc.tensor.matmul(z[:, dst[0], dst[1]:dst[1] + n], m[:], part_[src], start=False, stop=False, skip_group_check=True)
                    return mm

                def own(m, dst, n, src):
                    return add(m, dst, n, (sp_hi, sp_lo), (slice(None), src[0], slice(src[1], src[1] + n)))

                def summed(m, dst, n, src):
                    return add(m, dst, n, (sums_hi, sums_lo), (slice(None), src))
                n1, n2, n3 = (KT[j][2] for j in (1, 2, 3))
                own(tri, (0, 0), SEQ, (0, 0))
                own(tri, (2, 0), BANK_COLS[2], (2, 0))
                own(tri, (1, 0), n1, (1, 0))
                own(own_own, LAST, N_LAST, LAST)
                own(negones, (2, n2 - n3), n3 + DEC, KT[3][0:2])
                for cache in (S_CACHE0, S_CACHE1):
                    own(own_all, (2, cache[1] - META), N_LAST, LAST)
                summed(negones, (0, SEQ - n1), n1, S1)
                summed(negones, (1, n1 - n2), n2, S2)
                summed(cache_meta, S_OWN, DEC, CC).then_inc(cum_done, 1)

            def values(i, hh, first=False):
                r = slice(hh * HD, (hh + 1) * HD)
                head = 2 * i + hh
                if hh == 0:
                    pe.wait_ge(vtok_kept, i + 1)
                    pe.wait_ge(cv_loaded, 16 * (i + 1))
                    if not first:
                        pe.wait_ge(mix_done, i)
                pe.wait_ge(prob_done, 3 * head + 3)
                for n, (bank, off, cols, q0) in enumerate(KT):
                    nc.tensor.matmul(pv[r, q0:SEQ], v_tok[:, n, r], prob[:, bank, off:off + cols], start=(n == 0), stop=False, skip_group_check=True)
                nc.tensor.matmul(pv[r, SEQ - META:SEQ], v_tok[:, 4, r], prob[:, LAST[0], LAST[1]:LAST[1] + META], start=False, stop=True, skip_group_check=True)
                for n, ((bank, off), v) in enumerate(((S_CACHE0, cv_tok[:, 0, r]), (S_CACHE1, cv_tok[:, 1, r]), (S_OWN, v_tok[:, 4, r]))):
                    mm = nc.tensor.matmul(z[r, 1, S_PV:S_PV + DEC], v, prob[:, bank, off:off + DEC], start=(n == 0), stop=(n == 2), skip_group_check=True)
                mm.then_inc(pv_done, 1)

            def turn_back(src, slot):
                for t in range(5):
                    mm = nc.tensor.transpose(dense[:, slot, t // 4, (t % 4) * P:(t % 4 + 1) * P], src[:, t * P:(t + 1) * P], ident[:])
                return mm

            def keys_back(i, slot):
                pe.wait_ge(glu_done, i + 1)
                turn_back(kT, slot)
                return nc.tensor.transpose(dense[0:92, slot, 1, P:2 * P], conv_in[:, CTX_CACHE - PAD:CTX_S + DEC], ident[:])

            def cache_keys(i):
                pe.wait_ge(ck_loaded, 16 * (i + 1))
                for t in range(2):
                    mm = nc.tensor.transpose(dense[:, 0, 1, (2 + t) * P:(3 + t) * P], ck_tok[:, t, :], ident[:])
                return mm

            def turn(i, prev=None):
                first = prev is None

                def unit(u, slot, out_only=False):
                    pe.wait_ge(lo_done, LOOP_UNITS * i + u + 1)
                    dense_unit(u % RING_LOOP, slot, r_hi, r_lo, META if out_only else 0, HALFO if out_only else HALF)

                if first:
                    for u in range(2):
                        claim(u, X_EMPTIED[u])
                    for k in range(KC):
                        by_dve, by_pool = lows_before(k + 1)
                        if k in POOL_LOWS:
                            pe.wait_ge(r_ready_pool, by_pool)
                        else:
                            pe.wait_ge(r_ready, by_dve)
                        if k == 0:
                            pe.wait_ge(lo_done, 1)
                        q_end = passes(0, 0, r_hi, r_lo, META, HALFO, k)
                        if k == KC - 1:
                            q_end.then_inc(tile_done, 1)
                        if k == 0:
                            pe.wait_ge(lo_done, 2)
                        k_end = passes(1, 1, r_hi, r_lo, 0, HALF, k)
                    k_end.then_inc(tile_done, 1)
                else:
                    pe.wait_ge(gb_log, i)
                    unit(0, 0, True)
                    pe.wait_ge(ga_log, i)
                    unit(1, 1)
                pe.wait_ge(q_kept, i + 1)
                if not first:
                    keys_back(prev, 0)
                cache_keys(i).then_inc(tile_done, 1)
                if not first:
                    cumulate(2 * i - 1)
                pe.wait_ge(k_kept, i + 1)
                unit(2, 1)
                if not first:
                    values(prev, 1)
                scores(i, 0, first)
                if not first:
                    pe.wait_ge(ktok_kept, i)
                pe.wait_ge(v_kept, i + 1)
                turn_back(vT, 0).then_inc(tile_done, 1)
                unit(3, 1)
                pe.wait_ge(vtok_kept, i + 1)
                unit(4, 0)
                cumulate(2 * i)
                pe.wait_ge(a_kept, i + 1)
                unit(5, 1, True)
                values(i, 0, first)
                scores(i, 1)

            turn(0)
            with pe.Fori(0, KC - 1) as before:
                turn(before + 1, before)

            def unit(g, n, m_hi, m_lo, ready=None):
                pe.wait_ge(lo_done, N_LOOP + 4 * g + n + 1)
                claim(n % 2, X_EMPTIED[n % 2] + 2 * g + n // 2)
                dense_unit(n, n % 2, m_hi, m_lo, 0, HALFO, ready)

            def group(g, m_hi, m_lo, ready=None):
                for n in range(4):
                    unit(g, n, m_hi, m_lo, ready)

            def gate_conv(f):
                pe.wait_ge(lo_done, N_LOOP + f + 1)
                if f >= 3:
                    claim(f % 2, X_EMPTIED[f % 2] + f // 2)
                dense_unit(f % RING, f % 2, r_hi, r_lo, META, HALFO)

            pe.wait_ge(gb_log, KC)
            gate_conv(0)
            pe.wait_ge(ga_log, KC)
            gate_conv(1)
            claim(0, X_EMPTIED[0] + 1)
            keys_back(KC - 1, 0).then_inc(tile_done, 1)
            cumulate(2 * KC - 1)
            pe.wait_ge(ktok_kept, KC)
            gate_conv(2)
            values(KC - 1, 1)
            gate_conv(3)
            pe.wait_ge(sumy_done, KC)
            pe.wait_ge(mix_s_done, KC)
            for h in range(2):
                mm = nc.tensor.matmul(z[:, h, 0:HALFO], ones[:], sum_y[:, h * HALFO:(h + 1) * HALFO], start=True, stop=True)
            mm.then_inc(mean_done, 1)
            for f in (4, 5):
                gate_conv(f)
            pe.wait_ge(ssum_done, KC)
            for h in range(2):
                mm = nc.tensor.matmul(z[:, h, 0:HALFO], ones[:], sum_sq[:, h * HALFO:(h + 1) * HALFO], start=True, stop=True)
            mm.then_inc(var_done, 1)
            for f in (6, 7):
                gate_conv(f)
            with pe.Fori(2, 4) as g:
                group(g, s_hi, s_lo, (s_ready, 1))
            with pe.Fori(4, 6) as g:
                group(g, r_hi, r_lo, (m_ready, 1))

            u_parts = ((r_hi, r_lo), (u_hi, u_lo))
            unit(6, 0, s_hi, s_lo, (h2_ready, 1))
            pe.wait_ge(x2sum_done, KC)
            for h in range(2):
                mm = nc.tensor.matmul(z[:, h, 0:HALFO], ones[:], n32[:, 1, h * HALFO:(h + 1) * HALFO], start=True, stop=True)
            mm.then_inc(ss2_done, 1)
            for n in range(1, 4):
                unit(6, n, s_hi, s_lo)

            def tokens_back(f):
                pe.wait_ge(xg_done, f + 1)
                if f == 4:
                    pe.wait_ge(half_kept, 4)
                for t in range(4):
                    dst = pv if t == 3 else z[:, t]
                    mm = nc.tensor.transpose(dst[:, (f % 4) * P:(f % 4 + 1) * P], xT[:, f, META + t * P:META + (t + 1) * P], ident[:])
                mm.then_inc(turned, 1)

            def sample_back(f):
                pe.wait_ge(xg_done, f + 1)
                return nc.tensor.transpose(dense[0:DEC, 0, f // 4, (f % 4) * P:(f % 4 + 1) * P], xT[:, f, META + SEQ:], ident[:])

            for rr in range(2):
                with pe.Fori(7 if rr == 0 else 14, 10 + 8 * rr) as g:
                    group(g, s_hi, s_lo)
                with pe.Fori(10 + 8 * rr, 12 + 8 * rr) as g:
                    group(g, *u_parts[0], (u_ready, 16 * rr + 1))
                if rr == 0:
                    with pe.Fori(12, 14) as g:
                        group(g, *u_parts[1], (u_ready, KC + 1))
                else:
                    for f in range(KC):
                        unit(20 + f // 4, f % 4, *u_parts[1], (u_ready, 3 * KC + 1) if f == 0 else None)
                        if f >= 1:
                            tokens_back(f - 1)
            claim(0, X_EMPTIED[0] + 2 * N_GROUPS)
            for f in range(KC - 1):
                sample_back(f)
            tokens_back(KC - 1)
            sample_back(KC - 1).then_inc(turned, 1)
            claim(1, X_EMPTIED[1] + 2 * N_GROUPS)
            pe.wait_ge(x2sum_done, 2 * KC)
            for t in range(5):
                n = P if t < 4 else DEC
                mm = nc.tensor.matmul(dense[0:n, 1, 0, t:t + 1], n32[:, 1, t * P:t * P + n], ones[:, 0:1], start=(t == 0), stop=True, skip_group_check=True)
            mm.then_inc(ss2_done, 1)

        @block.scalar
        def _(act):
            def high(s, raw_sem, raw_count, free_tile):
                act.wait_ge(raw_sem, raw_count)
                if free_tile is not None:
                    act.wait_ge(tile_done, free_tile)
                nc.scalar.activation(w_hi[:, s], w_raw[:, s], ACT.Copy).then_inc(hi_done, 1)

            act.preload_act_table_set("natural_log_exp_and_others")
            for t in range(X_TILES):
                n = P if t < 4 else META + DEC
                act.wait_ge(x_loaded[t], 32 if t in (0, 4) else 16)
                if t >= 1:
                    act.wait_ge(sq_done, t)
                nc.scalar.activation(sq[0:n, :], x_tok[0:n, t, :], ACT.Square, accum_out=rstd_tok[0:n, t:t + 1]).then_inc(sq_done, 1)
            act.wait_ge(sq_done, X_TILES)
            act.wait_ge(eps_set, 1)
            LAST_TOK = META + DEC
            nc.scalar.activation(rstd_tok[:, 0:4], rstd_tok[:, 0:4], ACT.Ln, scale=1.0 / D, bias=eps_col[:, 0:1])
            nc.scalar.activation(rstd_tok[0:LAST_TOK, 4:5], rstd_tok[0:LAST_TOK, 4:5], ACT.Ln, scale=1.0 / D, bias=eps_col[0:LAST_TOK, 0:1]).then_inc(ln_step, 1)
            act.wait_ge(ln_step, 1)
            nc.scalar.activation(rstd_tok[:, 0:4], rstd_tok[:, 0:4], ACT.Exp, scale=-0.5)
            nc.scalar.activation(rstd_tok[0:LAST_TOK, 4:5], rstd_tok[0:LAST_TOK, 4:5], ACT.Exp, scale=-0.5).then_inc(root_done, 1)
            high(0, raw_loop[0], 16, None)
            act.wait_ge(rows_turned, 1)
            nc.scalar.activation(cw[:].rearrange("p k r -> p (k r)"), z[:, 0, 0:KC * 61], ACT.Copy).then_inc(rows_kept, 1)
            high(1, raw_loop[1], 16, None)
            act.wait_ge(spread, 1)
            nc.scalar.activation(rstd[:, 0:4 * P], z[:, 2], ACT.Copy)
            nc.scalar.activation(rstd[:, 4 * P:], pv[:, 0:TOK - 4 * P], ACT.Copy).then_inc(rstd_done, 1)

            def inverse_root(psum_sem, count, step, cols, half):
                act.wait_ge(psum_sem, count)
                nc.scalar.activation(cols2(rstd[:, 0:cols], half), z[:, 0:2, 0:half], ACT.Ln, scale=1.0 / D, bias=eps_col[:, 0:1]).then_inc(ln_step, 1)
                act.wait_ge(ln_step, step)
                nc.scalar.activation(rstd[:, 0:cols], rstd[:, 0:cols], ACT.Exp, scale=-0.5).then_inc(rstd_done, 1)

            def split_high(n, cols, ready, ready_count, dst, done):
                act.wait_ge(ready, ready_count)
                nc.scalar.activation(dst, n32[:, n % 2, 0:cols], ACT.Copy).then_inc(done, 1)

            for k in range(KC):
                split_high(k, TOK, n32_done, k + 1, r_hi[:, k, :], nhi_done)

            high(2, raw_loop[2], 16, None)

            def log_sigmoid_parts(src, dst, half, tile_n, s_abs, s_exp, s_ln, count):
                act.wait_ge(tile_done, tile_n)
                nc.scalar.activation(cols2(dst, half), src, ACT.Abs).then_inc(s_abs, 1)
                act.wait_ge(s_abs, count)
                nc.scalar.activation(dst, dst, ACT.Exp, scale=-1.0).then_inc(s_exp, 1)
                act.wait_ge(s_exp, count)
                nc.scalar.activation(dst, dst, ACT.Ln, bias=1.0).then_inc(s_ln, 1)

            def softplus_logs(head, between=None):
                def a(n):
                    b, c = BANKS[n], BANK_COLS[BANKS[n]]
                    act.wait_ge(z_scored, 3 * head + n + 1)
                    nc.scalar.activation(ez[:, b, 0:c], z[:, b, 0:c], ACT.Abs).then_inc(abs_done, 1)

                def e(n):
                    b, c = BANKS[n], BANK_COLS[BANKS[n]]
                    act.wait_ge(abs_done, 3 * head + n + 1)
                    nc.scalar.activation(ez[:, b, 0:c], ez[:, b, 0:c], ACT.Exp, scale=-1.0).then_inc(exp_done, 1)

                def l(n):
                    b, c = BANKS[n], BANK_COLS[BANKS[n]]
                    act.wait_ge(exp_done, 3 * head + n + 1)
                    nc.scalar.activation(ez[:, b, 0:c], ez[:, b, 0:c], ACT.Ln, bias=1.0).then_inc(log_done, 1)

                def h(n):
                    b, c = BANKS[n], BANK_COLS[BANKS[n]]
                    act.wait_ge(sp_done, 3 * head + n + 1)
                    nc.scalar.activation(sp_hi[:, b, 0:c], sp[:, b, 0:c], ACT.Copy).then_inc(sphi_done, 1)

                def hs(_):
                    act.wait_ge(sums_done, head + 1)
                    nc.scalar.activation(sums_hi, sums, ACT.Copy).then_inc(sumshi_done, 1)

                for step, n in ((a, 0), (a, 1), (e, 0), (a, 2), (e, 1), (l, 0), (e, 2), (l, 1), (l, 2), (h, 0), (h, 1), (h, 2), (hs, 0)):
                    if step is h and n == 0 and between is not None:
                        between()
                    step(n)

            def probabilities(head):
                act.wait_ge(cum_done, head + 1)
                for b in BANKS:
                    c = BANK_COLS[b]
                    nc.scalar.activation(prob[:, b, 0:c], z[:, b, 0:c], ACT.Exp).then_inc(prob_done, 1)

            def rows_out(buf, prompt, sample, i):
                n = bass.ds(i, 1)
                act.dma_start(prompt[0:4 * P, n, :].rearrange("(t p) n c -> p t (n c)", p=P), buf[:, 0:4, :]).then_inc(kv_out, 16)
                act.dma_start(prompt[4 * P:4 * P + META, n, :].rearrange("t n c -> t (n c)"), buf[0:META, 4, :]).then_inc(kv_out, 16)
                act.dma_start(sample[:, n, :].rearrange("t n c -> t (n c)"), buf[META:META + DEC, 4, :]).then_inc(kv_out, 16)

            def unturn(tile_n, dst, slot):
                act.wait_ge(tile_done, tile_n)
                nc.scalar.activation(dst[:, 0:4, :].rearrange("p t c -> p (t c)"), dense[:, slot, 0, :], ACT.Copy)
                return nc.scalar.activation(dst[:, 4, :], dense[:, slot, 1, 0:P], ACT.Copy)

            def attn_gate(i):
                log_sigmoid_parts(psum2(1, HALFO), gate_a[:], HALFO, tile(i, T_G) + 1, ga_abs, ga_exp, ga_ln, i + 1)

            def attn_gate_end(i):
                act.wait_ge(ga_log, i + 1)
                nc.scalar.activation(gate_a[:], gate_a[:], ACT.Exp).then_inc(ga_done, 1)

            def keys_out(i, tile_n, slot):
                act.wait_ge(kv_out, 16 * (8 * i + 3))
                unturn(tile_n, k_tok, slot)
                nc.scalar.activation(glu_tok[:], dense[0:92, slot, 1, P:2 * P], ACT.Copy).then_inc(ktok_kept, 1)
                act.wait_ge(ktok_kept, i + 1)
                rows_out(k_tok, nkp, nks, i)
                act.dma_start(ncp[:, bass.ds(i, 1), :].rearrange("t n c -> t (n c)"), glu_tok[0:PAD, :]).then_inc(kv_out, 16)
                act.dma_start(ncs[:, bass.ds(i, 1), :].rearrange("t n c -> t (n c)"), glu_tok[92 - PAD:92, :]).then_inc(kv_out, 16)

            def turn(i, prev=None):
                first = prev is None
                def high_ahead(u):
                    free = tile(i, UNIT_TILE[u - RING_LOOP]) + 1
                    high(u % RING_LOOP, raw_loop[u % LOOP_UNITS], 16 * (i + 1 + u // LOOP_UNITS), free)

                act.wait_ge(tile_done, tile(i, T_Q) + 1)
                nc.scalar.activation(cols2(q_hi[:], HALFO), psum2(0, HALFO), ACT.Copy, scale=HD ** -0.5)
                nc.scalar.activation(cols2(qT[:], HALFO), psum2(0, HALFO), ACT.Copy, scale=HD ** -0.5).then_inc(qhi_done, 1)
                if not first:
                    high_ahead(3)
                act.wait_ge(tile_done, tile(i, T_K) + 1)
                nc.scalar.activation(cols2(k_hi[:], HALF), psum2(1, HALF), ACT.Copy).then_inc(khi_done, 1)
                if first:
                    high_ahead(3)
                high_ahead(4)
                act.wait_ge(tile_done, tile(i, T_KC) + 1)
                nc.scalar.activation(ckT[:], dense[:, 0, 1, 2 * P:4 * P], ACT.Copy).then_inc(ckT_kept, 1)
                if not first:
                    keys_out(prev, tile(i, T_KC) + 1, 0)
                    probabilities(2 * i - 1)
                high_ahead(5)

                def values_out():
                    if not first:
                        act.wait_ge(kv_out, 16 * 8 * i)
                    unturn(tile(i, T_VT) + 1, v_tok, 0).then_inc(vtok_kept, 1)
                    act.wait_ge(vtok_kept, i + 1)
                    rows_out(v_tok, nvp, nvs, i)
                softplus_logs(2 * i, values_out)
                act.wait_ge(tile_done, tile(i, T_A) + 1)
                nc.scalar.activation(cols2(a_sb[:], HALF), psum2(1, HALF), ACT.Copy).then_inc(a_kept, 1)
                high_ahead(6)
                log_sigmoid_parts(psum2(0, HALF), gate_b[:], HALF, tile(i, T_B) + 1, gb_abs, gb_exp, gb_ln, i + 1)
                high_ahead(7)
                act.wait_ge(gb_log, i + 1)
                nc.scalar.activation(gate_b[:], gate_b[:], ACT.Exp).then_inc(gb_done, 1)
                probabilities(2 * i)
                attn_gate(i)
                high_ahead(8)
                attn_gate_end(i)
                softplus_logs(2 * i + 1)

            turn(0)
            with act.Fori(0, KC - 1) as before:
                turn(before + 1, before)

            def high_post(g, n):
                high((n + 2) % RING, raw_post[(n + 2) % RING], 16 * g if n == 0 else 16 * (g + 1), FIRST_POST + 4 * g + n - 1)

            def post_group(g, body):
                for n in range(4):
                    high_post(g, n)
                    body(n)

            def gate_conv(f, func, tile_n=None):
                act.wait_ge(tile_done, tile_n or FIRST_POST + f + 1)
                nc.scalar.activation(cols2(gate_c[:, f, :], HALFO), psum2(f % 2, HALFO), func).then_inc(emptied[f % 2], 1)

            def squares(ks):
                for k in ks:
                    act.wait_ge(centred, k + 1)
                    if k >= 2:
                        act.wait_ge(ssum_done, k - 1)
                    nc.scalar.activation(part[:, k % 2, :], yconv[:, k, :], ACT.Square).then_inc(ysq_done, 1)

            def silu(ks):
                for k in ks:
                    act.wait_ge(u_done, k + 1)
                    nc.scalar.activation(n32[:, k % 2, 0:OUTTOK], yconv[:, k, :], ACT.Silu, bias=vec(B_LN, k)).then_inc(silu_done, 1)
                    act.wait_ge(silu_done, k + 1)
                    nc.scalar.activation(s_hi[:, k, :], n32[:, k % 2, 0:OUTTOK], ACT.Copy).then_inc(nhi_done, 1)

            gate_conv(0, ACT.Copy, FIRST_POST)
            keys_out(KC - 1, FIRST_POST + 2, 0)
            probabilities(2 * KC - 1)
            high_post(0, 1)
            act.preload_act_table_set("sigmoid_and_others")
            gate_conv(1, ACT.Sigmoid, FIRST_POST + 1)
            high_post(0, 2)
            high_post(0, 3)
            gate_conv(2, ACT.Sigmoid)
            high_post(1, 0)
            gate_conv(3, ACT.Sigmoid)
            high_post(1, 1)
            squares(range(0, 5))
            gate_conv(4, ACT.Sigmoid)
            squares(range(5, KC))
            high_post(1, 2)
            act.preload_act_table_set("natural_log_exp_and_others")
            gate_conv(5, ACT.Copy)
            inverse_root(var_done, 1, 2, OUTTOK, HALFO)
            high_post(1, 3)
            act.wait_ge(kv_out, 16 * 8 * KC)
            act.preload_act_table_set("silu_and_others")
            silu(range(0, 4))
            gate_conv(6, ACT.Copy)
            silu(range(4, KC))
            gate_conv(7, ACT.Copy)
            for f in (0, 5, 6, 7):
                act.wait_ge(emptied[f % 2], X_EMPTIED[f % 2] + f // 2 + 1)
                nc.scalar.activation(gate_c[:, f, :], gate_c[:, f, :], ACT.Sigmoid).then_inc(gates_done, 1)

            def post(first, last, body):
                with act.Fori(first, last) as g:
                    post_group(g, lambda n: body(g, 4 * (g - first) + n, n))

            def merge(g, f, n):
                act.wait_ge(m_done, f + 1)
                nc.scalar.activation(r_hi[:, bass.ds(f, 1), 0:OUTTOK].rearrange("p n c -> p (n c)"), n32[:, n % 2, 0:OUTTOK], ACT.Copy).then_inc(mhi_done, 1)
            post(2, 4, merge)
            act.preload_act_table_set("natural_log_exp_and_others")

            def out_squares(g, f, n):
                fs = bass.ds(f, 1)
                x_cur = xT[:, fs, META:].rearrange("p n c -> p (n c)")
                act.wait_ge(emptied[n % 2], emptied_at(g, n))
                nc.scalar.activation(s_hi[:, fs, :].rearrange("p n c -> p (n c)"), x_cur, ACT.Copy, scale=vecs[:, bass.ds(G_MLP * KC + f, 1)]).then_inc(uhi_done, 1)
                nc.scalar.activation(n32[:, 0, 0:OUTTOK], x_cur, ACT.Square).then_inc(x2sq_done, 1)
                act.wait_ge(x2sum_done, f + 1)
            post(4, 6, out_squares)

            def up(g, f, n, half):
                U = 2 * KC * ((g0 - 6) // 8) + f
                act.wait_ge(emptied[n % 2], emptied_at(g, n))
                nc.scalar.activation(n32[:, n % 2, 0:OUTTOK], n32[:, n % 2, 0:OUTTOK], ACT.Square).then_inc(u32_done, 1)
                act.wait_ge(u32_done, U + 1)
                hi = (r_hi, u_hi)[half]
                nc.scalar.activation(hi[:, bass.ds(f - KC * half, 1), 0:OUTTOK].rearrange("p n c -> p (n c)"), n32[:, n % 2, 0:OUTTOK], ACT.Copy).then_inc(uhi_done, 1)

            for rr in range(2):
                g0 = 6 + 8 * rr
                if rr == 0:
                    high_post(6, 0)
                    inverse_root(ss2_done, 1, 3, OUTTOK, HALFO)
                    up(6, 0, 0, 0)
                    for n in range(1, 4):
                        high_post(6, n)
                        up(6, n, n, 0)
                with act.Fori(7 if rr == 0 else 14, g0 + 2) as g:
                    post_group(g, lambda n: up(g, 4 * (g - g0) + n, n, 0))
                with act.Fori(g0 + 2, g0 + 4) as g:
                    post_group(g, lambda n: up(g, 4 * (g - g0) + n, n, 1))
                if rr == 0:
                    with act.Fori(10, 14) as g:
                        post_group(g, lambda n: None)
            with act.Fori(18, 20) as g:
                post_group(g, lambda n: None)

            def half_back(t):
                act.wait_ge(turned, 4)
                nc.scalar.activation(y_tok[:, t, 0:D // 2], pv[:] if t == 3 else z[:, t], ACT.Copy).then_inc(half_kept, 1)

            for f in range(KC):
                g, n = 20 + f // 4, f % 4
                if f < KC - 2:
                    high_post(g, n)
                act.wait_ge(emptied[n % 2], emptied_at(g, n))
                if f >= 1:
                    act.wait_ge(x2sum_done, KC + f)
                nc.scalar.activation(n32[:, 0, 0:OUTTOK], xT[:, f, META:], ACT.Square).then_inc(x2sq_done, 1)
                act.wait_ge(x2sq_done, KC + f + 1)
                nc.scalar.activation(xT[:, f, META:], xT[:, f, META:], ACT.Copy, scale=vec(G_FINAL, f)).then_inc(xg_done, 1)
                if f == 4:
                    half_back(2)
                    half_back(3)
            act.wait_ge(ss2_done, 2)
            nc.scalar.activation(rstd_tok[:, 0:4], dense[:, 1, 0, 0:4], ACT.Ln, scale=1.0 / D, bias=eps_col[:, 0:1])
            nc.scalar.activation(rstd_tok[0:DEC, 4:5], dense[0:DEC, 1, 0, 4:5], ACT.Ln, scale=1.0 / D, bias=eps_col[0:DEC, 0:1]).then_inc(ln_step, 1)
            act.wait_ge(ln_step, 4)
            nc.scalar.activation(rstd_tok[:, 0:4], rstd_tok[:, 0:4], ACT.Exp, scale=-0.5)
            nc.scalar.activation(rstd_tok[0:DEC, 4:5], rstd_tok[0:DEC, 4:5], ACT.Exp, scale=-0.5).then_inc(rstd_done, 1)
            act.wait_ge(rstd_done, 4)
            for t in (2, 3):
                nc.scalar.activation(y_tok[:, t, D // 2:], pv[:] if t == 3 else z[:, t], ACT.Copy, scale=rstd_tok[:, t:t + 1]).then_inc(y_by_act, 1)
                nc.scalar.activation(y_tok[:, t, 0:D // 2], y_tok[:, t, 0:D // 2], ACT.Copy, scale=rstd_tok[:, t:t + 1]).then_inc(y_by_act, 1)
            nc.scalar.activation(y_tok[0:DEC, 4, D // 2:], dense[0:DEC, 0, 1, :], ACT.Copy, scale=rstd_tok[0:DEC, 4:5]).then_inc(y_by_act, 1)

        @block.vector
        def _(dve):
            nc.vector.memset(eps_col[:], EPS).then_inc(eps_set, 1)
            def keep_x(t):
                n = P if t < 4 else META + DEC
                dve.wait_ge(tile_done, t + 1)
                nc.vector.tensor_copy(xT[:, :, t * P:t * P + n], dense[:, t % 2].rearrange("p h (k c) -> p (h k) c", c=P)[:, :, 0:n]).then_inc(emptied[t % 2], 1)

            for t in range(3):
                keep_x(t)
            dve.wait_ge(root_done, 1)
            for t in range(X_TILES):
                n = P if t < 4 else META + DEC
                nc.vector.tensor_scalar(diag[0:n, t, 0:n], ident[0:n, 0:n], rstd_tok[0:n, t:t + 1], None, ALU.mult).then_inc(diag_done, 1)
            for t in (3, 4):
                keep_x(t)
            dve.wait_ge(rows_turned, 1)
            nc.vector.tensor_copy(vecs[:], z[:, 1, 0:6 * KC]).then_inc(rows_kept, 1)

            def normalise():
                for k in range(KC + 1):
                    if k < KC:
                        if k >= 2:
                            if k - 2 in POOL_LOWS:
                                dve.wait_ge(r_ready_pool, lows_before(k - 1)[1])
                            else:
                                dve.wait_ge(r_ready, lows_before(k - 1)[0])
                        nc.vector.scalar_tensor_tensor(n32[:, k % 2, :], xT[:, k, :], vec(G_MIX, k), rstd[:], ALU.mult, ALU.mult).then_inc(n32_done, 1)
                    if k >= 1 and k - 1 not in POOL_LOWS:
                        dve.wait_ge(nhi_done, k)
                        nc.vector.tensor_tensor(r_lo[:, k - 1, :], n32[:, (k - 1) % 2, :], r_hi[:, k - 1, :].bitcast(F32), ALU.subtract).then_inc(r_ready, 1)

            dve.wait_ge(rows_kept, 2)
            dve.wait_ge(emptied[0], X_EMPTIED[0])
            dve.wait_ge(rstd_done, 1)
            normalise()
            dve.wait_ge(zeroed, 4)

            def conv(i, taps):
                for k in taps:
                    src, w, dst = conv_in[:, META + k:META + k + CONV_COLS], cw_cur[:, PAD + k:PAD + k + 1], acc[:, k % 2, :]
                    if k < 2:
                        nc.vector.tensor_scalar(dst, src, w, None, ALU.mult).then_inc(tap_done, 1)
                    else:
                        dve.wait_ge(tap_done, TAPS * i + k - 1)
                        nc.vector.scalar_tensor_tensor(dst, src, w, dst, ALU.mult, ALU.add).then_inc(tap_done, 1)

            def gate_mix(i):
                mixed_cur = mixed[:, bass.ds(i, 1), :].rearrange("p n c -> p (n c)")
                dve.wait_ge(ga_done, i + 1)
                dve.wait_ge(pv_done, 2 * (i + 1))
                nc.vector.tensor_tensor(mixed_cur[:, SEQ:], z[:, 1, S_PV:S_PV + DEC], gate_a[:, SEQ:], ALU.mult).then_inc(mix_s_done, 1)
                nc.vector.tensor_tensor(mixed_cur[:, 0:SEQ], pv[:], gate_a[:, 0:SEQ], ALU.mult).then_inc(mix_done, 1)

            def attn_gate(i):
                dve.wait_ge(ga_ln, i + 1)
                nc.vector.scalar_tensor_tensor(cols2(gate_a[:], HALFO), psum2(1, HALFO), 0.0, cols2(gate_a[:], HALFO), ALU.min, ALU.subtract).then_inc(ga_log, 1)

            def conv_end(i):
                y_cur = yconv[:, bass.ds(i, 1), :].rearrange("p n c -> p (n c)")
                dve.wait_ge(tap_done, TAPS * (i + 1))
                nc.vector.scalar_tensor_tensor(y_cur[:, 0:SEQ], acc[:, 0, 0:SEQ], bdw_cur[:, 0:1], acc[:, 1, 0:SEQ], ALU.add, ALU.add)
                nc.vector.scalar_tensor_tensor(y_cur[:, SEQ:], acc[:, 0, CONV_COLS - DEC:], bdw_cur[:, 0:1], acc[:, 1, CONV_COLS - DEC:], ALU.add, ALU.add).then_inc(y_done, 1)
                dve.wait_ge(y_done, i + 1)
                nc.vector.tensor_tensor(sum_y[:], sum_y[:], y_cur, ALU.add).then_inc(sumy_done, 1)

            CONV = [range(a, b) for a, b in ((0, 8), (8, 11), (11, 12), (12, 13), (13, 16), (16, 24), (24, 27), (27, 28), (28, 29), (29, TAPS))]

            def turn(i, prev=None):
                first = prev is None
                def conv_before(n):
                    if not first:
                        conv(prev, CONV[n])

                def softplus_sum(head, n):
                    b, c = BANKS[n], BANK_COLS[BANKS[n]]
                    dve.wait_ge(log_done, 3 * head + n + 1)
                    nc.vector.scalar_tensor_tensor(sp[:, b, 0:c], z[:, b, 0:c], 0.0, ez[:, b, 0:c], ALU.max, ALU.add).then_inc(sp_done, 1)

                def softplus_low(head, n):
                    b, c = BANKS[n], BANK_COLS[BANKS[n]]
                    dve.wait_ge(sphi_done, 3 * head + n + 1)
                    nc.vector.tensor_tensor(sp_lo[:, b, 0:c], sp[:, b, 0:c], sp_hi[:, b, 0:c].bitcast(F32), ALU.subtract).then_inc(splo_done, 1)

                n1, n2, n3 = (KT[j][2] for j in (1, 2, 3))
                o3 = KT[3][1]

                def tile_sums(head):
                    dve.wait_ge(sp_done, 3 * head + 3)
                    nc.vector.tensor_copy(sums[:, S2.start:S2.start + n2 - n3], sp[:, 2, 0:n2 - n3])
                    nc.vector.tensor_tensor(sums[:, S2.stop - n3:S2.stop], sp[:, 2, n2 - n3:n2], sp[:, 2, o3:o3 + n3], ALU.add)
                    nc.vector.tensor_tensor(sums[:, CC], sp[:, 2, S_CACHE0[1]:S_CACHE0[1] + DEC], sp[:, 2, S_CACHE1[1]:S_CACHE1[1] + DEC], ALU.add)
                    nc.vector.tensor_copy(sums[:, 0:n1 - n2], sp[:, 1, 0:n1 - n2]).then_inc(sums_step, 1)
                    dve.wait_ge(sums_step, 2 * head + 1)
                    last = sums[:, S2.stop - META:S2.stop]
                    nc.vector.tensor_tensor(last, last, sp[:, 1, LAST[1]:LAST[1] + META], ALU.add).then_inc(sums_step, 1)
                    dve.wait_ge(sums_step, 2 * head + 2)
                    nc.vector.tensor_tensor(sums[:, n1 - n2:n1], sp[:, 1, n1 - n2:n1], sums[:, S2], ALU.add).then_inc(sums_done, 1)

                def sums_low(head):
                    dve.wait_ge(sumshi_done, head + 1)
                    nc.vector.tensor_tensor(sums_lo, sums, sums_hi.bitcast(F32), ALU.subtract).then_inc(splo_done, 1)

                def keep_keys(t, slot, dst, kept):
                    dve.wait_ge(tile_done, tile(i, t) + 1)
                    nc.vector.tensor_copy(cols2(dst[:, 0:TOK], HALF), psum2(slot, HALF))
                    nc.vector.tensor_copy(dst[:, TOK:TOK + META], dense[:, slot, 0, 0:META]).then_inc(kept, 1)

                dve.wait_ge(qhi_done, i + 1)
                nc.vector.scalar_tensor_tensor(cols2(q_lo[:], HALFO), psum2(0, HALFO), HD ** -0.5, cols2(q_hi[:].bitcast(F32), HALFO), ALU.mult, ALU.subtract).then_inc(q_kept, 1)
                conv_before(4)
                dve.wait_ge(khi_done, i + 1)
                nc.vector.tensor_tensor(cols2(k_lo[:], HALF), psum2(1, HALF), cols2(k_hi[:].bitcast(F32), HALF), ALU.subtract)
                dve.wait_ge(tile_done, tile(i, T_KC) + 1)
                nc.vector.tensor_copy(cols2(kT[:, 0:TOK], HALF), psum2(1, HALF))
                nc.vector.tensor_copy(kT[:, TOK:TOK + META], dense[:, 1, 0, 0:META]).then_inc(k_kept, 1)
                conv_before(5)
                keep_keys(T_V, 1, vT, v_kept)
                if not first:
                    gate_mix(prev)
                conv_before(6)
                for n in range(3):
                    softplus_sum(2 * i, n)
                    if n < 2:
                        conv_before(7 + n)
                tile_sums(2 * i)
                for n in range(3):
                    softplus_low(2 * i, n)
                sums_low(2 * i)
                conv_before(9)
                if not first:
                    conv_end(prev)
                n = bass.ds(i, 1)
                nc.vector.tensor_copy(cw_cur[:], cw[:, n, :].rearrange("p n c -> p (n c)"))
                nc.vector.tensor_copy(bdw_cur[:], vecs[:, bass.ds(B_DW * KC + i, 1)])
                nc.vector.tensor_copy(conv_in[:, CTX_CACHE:CTX_S], cw[:, n, 0:PAD].rearrange("p n c -> p (n c)")).then_inc(cur_done, 1)
                dve.wait_ge(gb_ln, i + 1)
                nc.vector.scalar_tensor_tensor(cols2(gate_b[:], HALF), psum2(0, HALF), 0.0, cols2(gate_b[:], HALF), ALU.min, ALU.subtract).then_inc(gb_log, 1)
                dve.wait_ge(gb_done, i + 1)
                nc.vector.tensor_tensor(conv_in[:, PAD:CTX_CACHE], a_sb[:, 0:META + SEQ], gate_b[:, 0:META + SEQ], ALU.mult)
                nc.vector.tensor_tensor(conv_in[:, CTX_S:], a_sb[:, META + SEQ:], gate_b[:, META + SEQ:], ALU.mult).then_inc(glu_done, 1)
                dve.wait_ge(glu_done, i + 1)
                dve.wait_ge(cur_done, i + 1)
                conv(i, CONV[0])
                attn_gate(i)
                conv(i, CONV[1])
                for n in range(3):
                    softplus_sum(2 * i + 1, n)
                    if n < 2:
                        conv(i, CONV[2 + n])
                tile_sums(2 * i + 1)
                for n in range(3):
                    softplus_low(2 * i + 1, n)
                sums_low(2 * i + 1)

            turn(0)
            with dve.Fori(0, KC - 1) as before:
                turn(before + 1, before)
            for taps in CONV[4:]:
                conv(KC - 1, taps)
            conv_end(KC - 1)
            gate_mix(KC - 1)

            nc.vector.memset(sum_sq[:], 0.0).then_inc(mean_kept, 1)
            dve.wait_ge(mean_done, 1)
            nc.vector.tensor_scalar(cols2(rstd[:, 0:OUTTOK], HALFO), z[:, 0:2, 0:HALFO], 1.0 / D, None, ALU.mult).then_inc(mean_kept, 1)
            dve.wait_ge(mean_kept, 2)
            for k in range(KC + 1):
                if k < KC:
                    nc.vector.tensor_tensor(yconv[:, k, :], yconv[:, k, :], rstd[:, 0:OUTTOK], ALU.subtract).then_inc(centred, 1)
                if k >= 1:
                    dve.wait_ge(ysq_done, k)
                    if k >= 2:
                        dve.wait_ge(ssum_done, k - 1)
                    nc.vector.tensor_tensor(sum_sq[:], sum_sq[:], part[:, (k - 1) % 2, :], ALU.add).then_inc(ssum_done, 1)
            dve.wait_ge(rstd_done, 2)
            for k in range(KC + 1):
                if k < KC:
                    nc.vector.scalar_tensor_tensor(yconv[:, k, :], yconv[:, k, :], vec(G_LN, k), rstd[:, 0:OUTTOK], ALU.mult, ALU.mult).then_inc(u_done, 1)
                if k >= 1:
                    dve.wait_ge(nhi_done, KC + k)
                    nc.vector.tensor_tensor(s_lo[:, k - 1, :], n32[:, (k - 1) % 2, 0:OUTTOK], s_hi[:, k - 1, :].bitcast(F32), ALU.subtract).then_inc(s_ready, 1)

            with dve.Fori(2, 4) as g:
                for n in range(4):
                    f = 4 * (g - 2) + n
                    fs = bass.ds(f, 1)
                    flat = "p n c -> p (n c)"
                    dve.wait_ge(tile_done, FIRST_POST + 4 * g + n + 1)
                    if n == 0:
                        dve.wait_ge(gates_done, 4)
                    nc.vector.tensor_tensor(cols2(part[:, n % 2, :], HALFO), psum2(n % 2, HALFO), cols2(gate_c[:, fs, :].rearrange(flat), HALFO), ALU.mult)\
                        .then_inc(emptied[n % 2], 1)
                    dve.wait_ge(emptied[n % 2], emptied_at(g, n))
                    nc.vector.tensor_tensor(n32[:, n % 2, 0:OUTTOK], part[:, n % 2, :], mixed[:, fs, :].rearrange(flat), ALU.add).then_inc(m_done, 1)
                    dve.wait_ge(mhi_done, f + 1)
                    nc.vector.tensor_tensor(r_lo[:, fs, 0:OUTTOK].rearrange(flat), n32[:, n % 2, 0:OUTTOK], r_hi[:, fs, 0:OUTTOK].rearrange(flat).bitcast(F32), ALU.subtract)\
                        .then_inc(m_ready, 1)

            def residual(tile_n, slot, x_cur):
                dve.wait_ge(tile_done, tile_n)
                nc.vector.tensor_tensor(cols2(x_cur, HALFO), psum2(slot, HALFO), cols2(x_cur, HALFO), ALU.add).then_inc(emptied[slot], 1)

            def add_square(count):
                dve.wait_ge(x2sq_done, count)
                nc.vector.tensor_tensor(n32[:, 1, 0:OUTTOK], n32[:, 1, 0:OUTTOK], n32[:, 0, 0:OUTTOK], ALU.add).then_inc(x2sum_done, 1)

            dve.wait_ge(m_ready, KC)
            nc.vector.memset(n32[:, 1, :], 0.0).then_inc(mean_kept, 1)
            dve.wait_ge(mean_kept, 3)
            with dve.Fori(4, 6) as g:
                for n in range(4):
                    f = 4 * (g - 4) + n
                    fs = bass.ds(f, 1)
                    x_cur = xT[:, fs, META:].rearrange("p n c -> p (n c)")
                    residual(FIRST_POST + 4 * g + n + 1, n % 2, x_cur)
                    dve.wait_ge(uhi_done, f + 1)
                    nc.vector.scalar_tensor_tensor(s_lo[:, fs, :].rearrange("p n c -> p (n c)"), x_cur, vecs[:, bass.ds(G_MLP * KC + f, 1)],
                                                   s_hi[:, fs, :].rearrange("p n c -> p (n c)").bitcast(F32), ALU.mult, ALU.subtract).then_inc(h2_ready, 1)
                    add_square(f + 1)

            def up(g, g0, n, half):
                f = 4 * (g - g0) + n
                U = 2 * KC * ((g0 - 6) // 8) + f
                tile_n = FIRST_POST + 4 * g + n + 1
                dve.wait_ge(tile_done, tile_n)
                nc.vector.scalar_tensor_tensor(cols2(n32[:, n % 2, 0:OUTTOK], HALFO), psum2(n % 2, HALFO), 0.0, cols2(rstd[:, 0:OUTTOK], HALFO), ALU.max, ALU.mult)\
                    .then_inc(emptied[n % 2], 1)
                dve.wait_ge(uhi_done, KC + U + 1)
                fs = bass.ds(f - KC * half, 1)
                hi, lo = ((r_hi, r_lo), (u_hi, u_lo))[half]
                nc.vector.tensor_tensor(lo[:, fs, 0:OUTTOK].rearrange("p n c -> p (n c)"), n32[:, n % 2, 0:OUTTOK],
                                        hi[:, fs, 0:OUTTOK].rearrange("p n c -> p (n c)").bitcast(F32), ALU.subtract).then_inc(u_ready, 1)

            dve.wait_ge(rstd_done, 3)
            for rr in range(2):
                g0 = 6 + 8 * rr
                for half in range(2):
                    with dve.Fori(g0 + 2 * half, g0 + 2 * half + 2) as g:
                        for n in range(4):
                            up(g, g0, n, half)
                for half in range(2 if rr == 0 else 1):
                    with dve.Fori(g0 + 4 + 2 * half, g0 + 6 + 2 * half) as g:
                        for n in range(4):
                            f = 4 * (g - g0 - 4 - 2 * half) + n
                            residual(FIRST_POST + 4 * g + n + 1, n % 2, xT[:, bass.ds(f, 1), META:].rearrange("p n c -> p (n c)"))
            dve.wait_ge(u_ready, 4 * KC)
            nc.vector.memset(n32[:, 1, :], 0.0).then_inc(mean_kept, 1)
            dve.wait_ge(mean_kept, 4)
            for f in range(KC):
                residual(FIRST_POST + 4 * 20 + f + 1, f % 2, xT[:, f, META:])
                add_square(KC + f + 1)
                if f == 4:
                    dve.wait_ge(turned, 4)
                    for t in (0, 1):
                        nc.vector.tensor_copy(y_tok[:, t, 0:D // 2], z[:, t]).then_inc(half_kept, 1)
            dve.wait_ge(rstd_done, 4)
            dve.wait_ge(half_kept, 4)
            dve.wait_ge(turned, KC + 1)
            for t in (0, 1):
                nc.vector.tensor_scalar(y_tok[:, t, D // 2:], z[:, t], rstd_tok[:, t:t + 1], None, ALU.mult).then_inc(y_by_dve, 1)
                nc.vector.tensor_scalar(y_tok[:, t, 0:D // 2], y_tok[:, t, 0:D // 2], rstd_tok[:, t:t + 1], None, ALU.mult).then_inc(y_by_dve, 1)
            nc.vector.tensor_scalar(y_tok[0:DEC, 4, 0:D // 2], dense[0:DEC, 0, 0, :], rstd_tok[0:DEC, 4:5], None, ALU.mult).then_inc(y_by_dve, 1)


_INS = ["x_prompt", "x_sample", "cache_k", "cache_v", "cache_conv", "meta", "g_mix", "w_in", "w_dw", "b_dw",
        "g_ln_conv", "b_ln_conv", "w_pw2", "w_out", "g_mlp", "w_up", "w_down", "g_final"]
_OUTS = [(1, SEQ, D), (1, DEC, D), (1, 1, META + SEQ, HEADS, HD), (1, 1, META + SEQ, HEADS, HD), (1, 1, PAD, D),
         (1, 1, DEC, HEADS, HD), (1, 1, DEC, HEADS, HD), (1, 1, PAD, D)]


def kernel(**inputs):
    import numpy as _np
    import concourse.bacc as _bacc
    from concourse.bass_utils import run_bass_kernel_spmd as _run

    nc = _bacc.Bacc("TRN2", target_bir_lowering=False, num_devices=1)
    arrays, args = {}, []
    for name in _INS:
        a = _np.ascontiguousarray(inputs[name])
        arrays[f"in_{name}_dram"] = a
        args.append(nc.dram_tensor(f"in_{name}_dram", a.shape, mybir.dt.from_np(a.dtype), kind="ExternalInput").ap())
    for n, shape in enumerate(_OUTS):
        args.append(nc.dram_tensor(f"out_{n}_dram", shape, F32, kind="ExternalOutput").ap())
    build(nc, *args)
    r = _run(nc, [arrays], core_ids=[0])
    return tuple(r.results[0][f"out_{n}_dram"] for n in range(len(_OUTS)))
```
